# Optimizing a Trainium2 kernel written in Bass

```python
import math
import jax, jax.numpy as jnp
from jax import lax
import numpy as np

D_MODEL = 2048
BATCH = 1
SEQ = 256
DEPTH = 1
DEC_BATCH = 8
DEC_SEQ = 4
PAST_LEN = 2048
PAGE_SIZE = 128

D_A = D_MODEL
H_A = 8
DH_A = D_A // H_A
D_B = D_MODEL
G_B = 8
CHUNK = 128
CONV_W = 4
EPS = 1e-6

COLUMN_SPLITS = (("q", D_A), ("k", D_A), ("v", D_A), ("o", D_A), ("za", D_A),
                 ("ig", H_A), ("fg", H_A),
                 ("u", D_B), ("vb", D_B), ("zb", D_B),
                 ("ga", D_MODEL), ("gb", D_MODEL))

kernel_name = "hybrid_mlstm_gmlp_gated_decode_step"

def _n_cols():
    return sum(w for _, w in COLUMN_SPLITS)

def _split_columns(p):
    idx = np.cumsum([w for _, w in COLUMN_SPLITS])[:-1].tolist()
    return jnp.split(p, idx, axis=-1)

def _rmsnorm(x, g):
    xf = x.astype(jnp.float32)
    y = xf * lax.rsqrt(jnp.mean(xf * xf, axis=-1, keepdims=True) + EPS) * g.astype(jnp.float32)
    return y.astype(x.dtype)

def _layernorm(x, g, b):
    xf = x.astype(jnp.float32)
    mu = jnp.mean(xf, axis=-1, keepdims=True)
    xc = xf - mu
    y = xc * lax.rsqrt(jnp.mean(xc * xc, axis=-1, keepdims=True) + EPS) * g.astype(jnp.float32) + b.astype(jnp.float32)
    return y.astype(x.dtype)

def _causal_conv(x, buf, w, b):
    T = x.shape[1]
    xp = jnp.concatenate([buf.astype(x.dtype), x], axis=1)
    out = b
    for j in range(CONV_W):
        out = out + w[j] * xp[:, j:j + T]
    return out, xp[:, T:]

def _mlstm_chunkwise(q, k, v, ig, lf, C0, n0, m0):
    B, T, H, D = q.shape
    L = math.gcd(T, CHUNK)
    nc = T // L

    def to_chunks(a):
        return jnp.moveaxis(a.reshape((B, nc, L) + a.shape[2:]), 1, 0)

    xs = tuple(to_chunks(a) for a in (q, k, v, ig, lf))
    causal = jnp.tril(jnp.ones((L, L), dtype=bool))

    def step(carry, inp):
        C, n, m = carry
        qb, kb, vb, ib, fb = inp
        bcum = jnp.cumsum(fb, axis=1)
        dmat = bcum[:, :, None, :] - bcum[:, None, :, :] + ib[:, None, :, :]
        dmat = jnp.where(causal[None, :, :, None], dmat, -jnp.inf)
        inter = bcum + m[:, None, :]
        m_row = jnp.maximum(jnp.max(dmat, axis=2), inter)
        wts = jnp.exp(dmat - m_row[:, :, None, :])
        sc_inter = jnp.exp(inter - m_row)
        s = jnp.einsum('bthd,bshd->btsh', qb, kb) * wts
        num = (jnp.einsum('btsh,bshd->bthd', s, vb)
               + sc_inter[..., None] * jnp.einsum('bhvk,bthk->bthv', C, qb))
        den = jnp.sum(s, axis=2) + sc_inter * jnp.einsum('bhk,bthk->bth', n, qb)
        h = num / jnp.maximum(jnp.abs(den), jnp.exp(-m_row))[..., None]
        b_last = bcum[:, -1]
        src = b_last[:, None, :] - bcum + ib
        m_new = jnp.maximum(b_last + m, jnp.max(src, axis=1))
        ws = jnp.exp(src - m_new[:, None, :])
        decay = jnp.exp(b_last + m - m_new)
        C_new = decay[..., None, None] * C + jnp.einsum('bsh,bshv,bshk->bhvk', ws, vb, kb)
        n_new = decay[..., None] * n + jnp.einsum('bsh,bshk->bhk', ws, kb)
        return (C_new, n_new, m_new), h

    (C, n, m), hs = lax.scan(step, (C0, n0, m0), xs)
    h = jnp.moveaxis(hs, 0, 1).reshape(B, T, H, D)
    return h, C, n, m

def _spatial_gating(u, v, w_s, b_s):
    B, T, _ = v.shape
    L = min(T, CHUNK)
    nc = T // L
    vg = v.reshape(B, nc, L, G_B, D_B // G_B)
    w = w_s[:, :L, :L] * jnp.tril(jnp.ones((L, L), dtype=w_s.dtype))
    s = jnp.einsum('gts,bnsgc->bntgc', w, vg) + b_s[:, :L].T[None, None, :, :, None]
    return u * s.reshape(B, T, D_B)

def _layer(x, conv_buf, C0, n0, m0, g_pre, w_in, b_ig, b_fg, w_conv, b_conv, g_head,
           ln_g, ln_b, w_s, b_s, w_pa, w_pb, w_out, g_post):
    B, T, _ = x.shape
    h = _rmsnorm(x, g_pre)
    proj = jnp.einsum('btd,dn->btn', h, w_in)
    q_pre, k_pre, v_a, o_pre, za, ig_pre, fg_pre, u, vb, zb, ga, gb = _split_columns(proj)

    qk_pre = jnp.concatenate([q_pre, k_pre], axis=-1)
    qk, conv_new = _causal_conv(qk_pre, conv_buf, w_conv, b_conv)
    qk = jax.nn.silu(qk).astype(jnp.float32)
    q = qk[..., :D_A].reshape(B, T, H_A, DH_A)
    k = qk[..., D_A:].reshape(B, T, H_A, DH_A) * (DH_A ** -0.5)
    v = v_a.astype(jnp.float32).reshape(B, T, H_A, DH_A)
    ig = ig_pre.astype(jnp.float32) + b_ig.astype(jnp.float32)
    lf = jax.nn.log_sigmoid(fg_pre.astype(jnp.float32) + b_fg.astype(jnp.float32))
    h_cell, C, n, m = _mlstm_chunkwise(q, k, v, ig, lf, C0.astype(jnp.float32),
                                       n0.astype(jnp.float32), m0.astype(jnp.float32))
    hn = h_cell * lax.rsqrt(jnp.mean(h_cell * h_cell, axis=-1, keepdims=True) + EPS) * g_head.astype(jnp.float32)
    hn = hn.reshape(B, T, D_A).astype(x.dtype)
    y_a = jax.nn.sigmoid(o_pre) * hn * jax.nn.silu(za)

    vb_n = _layernorm(vb, ln_g, ln_b)
    y_b = _spatial_gating(u, vb_n, w_s, b_s) * jax.nn.silu(zb)

    merged = (jax.nn.sigmoid(ga) * jnp.einsum('btc,cd->btd', y_a, w_pa)
              + jax.nn.sigmoid(gb) * jnp.einsum('btc,cd->btd', y_b, w_pb))
    out = jnp.einsum('btd,de->bte', merged, w_out)
    y = x + _rmsnorm(out, g_post)
    start = ((T - 1) // CHUNK) * CHUNK
    vrows = vb_n[:, start:]
    dt = x.dtype
    return y, C.astype(dt), n.astype(dt), m.astype(dt), conv_new.astype(dt), vrows

def setup_inputs(seed: int = 0) -> dict:
    key = jax.random.key(seed)
    ks = jax.random.split(key, 24)
    f32 = jnp.float32
    nrm = lambda k, s, sc: (jax.random.normal(k, s, f32) * sc)
    n_cols = _n_cols()
    return {
        "x_prompt": nrm(ks[0], (BATCH, SEQ, D_MODEL), 1.0),
        "x_sample": nrm(ks[1], (DEC_BATCH, DEC_SEQ, D_MODEL), 1.0),
        "state_mlstm_C": nrm(ks[2], (DEC_BATCH, H_A, DH_A, DH_A), DH_A ** -0.5),
        "state_mlstm_n": nrm(ks[3], (DEC_BATCH, H_A, DH_A), DH_A ** -0.5),
        "state_mlstm_m": nrm(ks[4], (DEC_BATCH, H_A), 1.0),
        "state_conv_qk": nrm(ks[5], (DEC_BATCH, CONV_W - 1, 2 * D_A), 1.0),
        "g_pre": 1.0 + nrm(ks[6], (D_MODEL,), 0.05),
        "w_in": nrm(ks[7], (D_MODEL, n_cols), D_MODEL ** -0.5),
        "b_ig": nrm(ks[8], (H_A,), 0.1),
        "b_fg": jnp.linspace(3.0, 6.0, H_A, dtype=f32) + nrm(ks[9], (H_A,), 0.1),
        "w_conv": nrm(ks[10], (CONV_W, 2 * D_A), CONV_W ** -0.5),
        "b_conv": nrm(ks[11], (2 * D_A,), 0.02),
        "g_head": 1.0 + nrm(ks[12], (H_A, DH_A), 0.05),
        "ln_g": 1.0 + nrm(ks[13], (D_B,), 0.05),
        "ln_b": nrm(ks[14], (D_B,), 0.02),
        "w_s": nrm(ks[15], (G_B, CHUNK, CHUNK), 0.5 * CHUNK ** -0.5),
        "b_s": 1.0 + nrm(ks[16], (G_B, CHUNK), 0.1),
        "w_pa": nrm(ks[17], (D_A, D_MODEL), D_A ** -0.5),
        "w_pb": nrm(ks[18], (D_B, D_MODEL), D_B ** -0.5),
        "w_out": nrm(ks[19], (D_MODEL, D_MODEL), D_MODEL ** -0.5),
        "g_post": 1.0 + nrm(ks[20], (D_MODEL,), 0.05),
    }

def reference(x_prompt, x_sample, state_mlstm_C, state_mlstm_n, state_mlstm_m, state_conv_qk,
              g_pre, w_in, b_ig, b_fg, w_conv, b_conv, g_head, ln_g, ln_b, w_s, b_s,
              w_pa, w_pb, w_out, g_post):
    dt = x_prompt.dtype
    C0 = jnp.zeros((BATCH, H_A, DH_A, DH_A), dt)
    n0 = jnp.zeros((BATCH, H_A, DH_A), dt)
    m0 = jnp.zeros((BATCH, H_A), dt)
    buf0 = jnp.zeros((BATCH, CONV_W - 1, 2 * D_A), dt)
    y_prompt, x_p, n_p, m_p, conv_p, vrows_p = x_prompt, None, None, None, None, None
    y_sample = x_sample
    for _ in range(DEPTH):
        y_prompt, C_p, n_p, m_p, conv_p, vrows_p = _layer(
            y_prompt, buf0, C0, n0, m0, g_pre, w_in, b_ig, b_fg, w_conv, b_conv, g_head,
            ln_g, ln_b, w_s, b_s, w_pa, w_pb, w_out, g_post)
        y_sample, C_s, n_s, m_s, conv_s, vrows_s = _layer(
            y_sample, state_conv_qk, state_mlstm_C, state_mlstm_n, state_mlstm_m,
            g_pre, w_in, b_ig, b_fg, w_conv, b_conv, g_head,
            ln_g, ln_b, w_s, b_s, w_pa, w_pb, w_out, g_post)
    return (y_prompt, y_sample, C_p, n_p, m_p, conv_p, vrows_p, C_s, n_s, m_s, conv_s, vrows_s)


_drawn_inputs = setup_inputs


def setup_inputs(seed=0):
    import zlib

    import numpy as np

    out = dict(_drawn_inputs(seed))
    spreads = {}
    factors = {'g_head': 3.454, 'ln_b': 2.792}
    for name, (base, spread) in spreads.items():
        noise = np.random.default_rng([zlib.crc32(name.encode()), seed]).standard_normal(out[name].shape)
        drawn = base * np.exp(spread * noise) if base else spread * noise
        out[name] = __import__('jax').numpy.asarray(drawn.astype(out[name].dtype))
    for name, factor in factors.items():
        out[name] = (out[name] * factor).astype(out[name].dtype)
    return out
```

```python
import concourse.bass as bass
from concourse import mybir

F32 = mybir.dt.float32
F32R = mybir.dt.float32r
ALU = mybir.AluOpType
ACT = mybir.ActivationFunctionType
ds = bass.ds

P = 128
D = 2048
KT = D // P
HEADS, DH = 8, 256
GROUPS = 8
TP, NB, TS = 256, 8, 4
S = NB * TS
T = TP + S
PW = 256
CK = 4
CHUNKS = KT // CK
CONV = 4
HIST = CONV - 1
XPS = HIST + TP
XPW = XPS + NB * (HIST + TS)
CW = XPW - HIST
NEW_BANK = (2, 3, 5)
EPS = 1e-6
MASKED = -30000.0
NEVER = -3.0e38

COL_Q, COL_K, COL_V, COL_O, COL_ZA = (D * i for i in range(5))
COL_IG = 5 * D
COL_U = COL_IG + 2 * HEADS
COL_VB, COL_ZB, COL_GA, COL_GB = (COL_U + D * i for i in range(1, 5))

V0, G0, MB0, H0, MA0, O0 = 0, 8, 24, 40, 80, 96
V_USE, G_USE, MB_USE, H_USE, MA_USE, O_USE = (0, 0), (4, 4), (12, 12), (20, 20), (44, 36), (52, 44)
PAIRS = 104


class Steps:

    def __init__(self, eng, sem, before=0):
        self.eng, self.sem, self.before, self.n = eng, sem, before, 0

    def __call__(self, ins):
        self.n += 1
        ins.then_inc(self.sem, 1)
        self.eng.wait_ge(self.sem, self.before + self.n)


def build(nc, x_prompt, x_sample, state_C, state_n, state_m, state_conv, g_pre, w_in, b_ig, b_fg,
          w_conv, b_conv, g_head, ln_g, ln_b, w_s, b_s, w_pa, w_pb, w_out, g_post,
          y_prompt, y_sample, C_p, n_p, m_p, conv_p, vrows_p, C_s, n_s, m_s, conv_s, vrows_s):

    base = (nc.sbuf_base + 63) // 64 * 64
    limit = nc.sbuf_usable_end

    class Area:
        def __init__(self, start):
            self.at = start

        def __call__(self, name, shape, dt=F32):
            n = 4
            for s in shape[1:]:
                n *= s
            t = nc.alloc_sbuf_tensor_at(name, shape, dt, offset=self.at)
            self.at += (n + 31) // 32 * 32
            assert self.at <= limit, (name, self.at, limit)
            return t

    fixed = Area(base)
    xh = fixed("xh", [P, KT, T], F32R)
    xl = fixed("xl", [P, KT, T], F32R)
    raw = fixed("raw", [P, CHUNKS, CK, PW])
    whi = fixed("whi", [P, CHUNKS, CK, PW], F32R)
    wlo = fixed("wlo", [P, CHUNKS, CK, PW], F32R)
    ident = fixed("ident", [P, P])
    keep_w = fixed("keep_w", [P, P + S])
    mask8 = fixed("mask8", [P, NB])
    rep32 = fixed("rep32", [S, P])
    eye8 = fixed("eye8", [HEADS, HEADS])
    par0 = fixed("par0", [P, P])
    par1 = fixed("par1", [P, 64])
    ghh = fixed("ghh", [P, 16])
    rstd = fixed("rstd", [P, 3])
    stat = fixed("stat", [P, 3])
    gq = fixed("gq", [P, 3, 96])
    nb = fixed("nb", [HEADS, T + S])
    dec_bc = fixed("dec_bc", [P, HEADS * NB])
    decT = fixed("decT", [NB, HEADS])
    nTh = fixed("nTh", [P, 2, NB * HEADS], F32R)
    nTl = fixed("nTl", [P, 2, NB * HEADS], F32R)
    half = fixed("half", [P, 3])
    onesrow = fixed("onesrow", [1, P])
    yarea = fixed.at
    y_ = Area(yarea)
    yh = y_("yh", [P, KT, T], F32R)
    yl = y_("yl", [P, KT, T], F32R)
    phase = y_.at

    a = Area(phase)
    xt = a("xt", [P, 3, D])
    hb0 = a("hb0", [P, 3, D])
    prow = a("prow", [P, 2, P])
    a = Area(phase)
    vtok = a("vtok", [P, 3, D])
    lng = a("lng", [P, D])
    lnb = a("lnb", [P, D])
    wsn = a("wsn", [P, GROUPS, P])
    brow = a("brow", [1, GROUPS, P])
    a = Area(max(a.at, phase + 2 * 3 * D * 4 + 1024 + 64))
    wsT = a("wsT", [P, GROUPS, P])
    b = Area(a.at)
    vf = b("vf", [P, 2, 2, T])
    vn = b("vn", [P, 3, DH])
    uf = b("uf", [P, 2, T])
    zs_g = b("zs_g", [P, 2, T])
    tt_g = b("tt_g", [P, 2, T])
    yf_g = b("yf_g", [P, 2, T])
    rep4 = b("rep4", [TS, S])
    wd = b("wd", [S, GROUPS, S])
    tri01 = b("tri01", [P, P])
    blk01 = b("blk01", [S, S])
    vstat = b("vstat", [P, 3, 8, 6])
    mv = b("mv", [P, 3, 2])
    nmu = b("nmu", [P, 3])
    ypost_end = b.at
    g = Area(yarea)
    wg = g("wg", [P, KT, 16])
    wgh = g("wgh", [P, KT, 40], F32R)
    wgl = g("wgl", [P, KT, 40], F32R)
    bg = g("bg", [HEADS, 2])
    m0 = g("m0", [HEADS, NB])
    nrow = g("nrow", [NB * HEADS, DH])
    r01 = g("r01", [HEADS, T])
    rneg = g("rneg", [HEADS, T])
    gf = g("gf", [HEADS, T])
    gab = g("gab", [HEADS, T])
    gln = g("gln", [HEADS, T])
    glf = g("glf", [HEADS, T])
    gbc = g("gbc", [HEADS, T])
    ga_ = g("ga_", [HEADS, T])
    gd1 = g("gd1", [HEADS, T])
    gM = g("gM", [HEADS, T])
    gx = g("gx", [HEADS, 2 * T + S + NB])
    gy = g("gy", [HEADS, 2 * T + S + NB])
    gqs = g("gqs", [96, T])
    gdx = g("gdx", [HEADS, HEADS, NB])
    gmn = g("gmn", [HEADS, 1 + NB])
    ones8 = g("ones8", [HEADS, P])
    assert g.at <= phase
    a = Area(phase)
    part = a("part", [P, KT, T])
    after_part = a.at
    a = Area(after_part)
    Cin = a("Cin", [P, NB, 2, DH])
    CTh = a("CTh", [P, 2, DH + 2], F32R)
    CTl = a("CTl", [P, 2, DH + 2], F32R)
    ktok = a("ktok", [P, 3, DH])
    vtok_h = a("vtok_h", [P, 3, DH + 1])
    kst = a("kst", [P, DH], F32R)
    vst = a("vst", [P, DH], F32R)
    W = a("W", [P, 416])
    scb = a("scb", [P, 2, S])
    qk = a("qk", [P, 4, T])
    vm = nc.alloc_sbuf_tensor_at("vm", [P, 4, XPW], F32R, offset=a.at)[:, :, 4:4 + DH]
    xp = a("xp", [P, 4, XPW])
    hb = a("hb", [P, 3, DH])
    acc = hb[:].rearrange("p t d -> p (t d)")[:, 0:2 * XPW].rearrange("p (j c) -> p j c", j=2)
    vz = a("vz", [P, 2, T])
    og = a("og", [P, 2, T])
    tg = og
    yf = og
    qm = a("qm", [P, 2, S + NB * (2 * S + TS)], F32R)
    cpo = a("cpo", [P, 2, DH])
    cn = a("cn", [P, 4, 27])
    cst = a("cst", [27, 4, P])
    hst = a("hst", [24, 2, DH])
    nin = a("nin", [NB, DH])
    nout = a("nout", [NB, 2, DH])
    bcrow = a("bcrow", [HEADS, T + S])
    ones8h = a("ones8h", [HEADS, P])
    r3 = a("r3", [P, 3])
    q3 = a("q3", [P, 3])
    f3 = a("f3", [P, 3])
    a = Area(after_part)
    tm = a("tm", [P, 2, T])
    sm = a("sm", [P, 2, T])
    mh = a("mh", [P, KT, T], F32R)
    ml = a("ml", [P, KT, T], F32R)
    a = Area(phase)
    vf_o = a("vf_o", [P, 2, 2, T])
    assert a.at <= after_part
    a = Area(yarea)
    otok = a("otok", [P, 3, D])
    gpost = a("gpost", [P, D])
    assert a.at <= phase
    xres = Area(base)("xres", [P, 3, D])
    ostat = Area(phase + 2 * 2 * T * 4 * 2)("ostat", [P, 3, 8, 6])
    omv = Area(phase + 2 * 2 * T * 4 * 2 + 1024)("omv", [P, 3, 2])

    ps = nc.alloc_psum_tensor("ps", [P, 8, 512], F32)

    def sem(name):
        return nc.alloc_semaphore(name)

    raw_landed = [sem(f"raw_landed{c}") for c in range(CHUNKS)]
    hi_ready, lo_ready, chunk_done = sem("hi_ready"), sem("lo_ready"), sem("chunk_done")
    slot_free = [sem("slot0_free"), sem("slot1_free")]
    x_in, par_in, gin, w_sp_in, ln_in = sem("x_in"), sem("par_in"), sem("gin"), sem("w_sp_in"), sem("ln_in")
    consts, const_v, par_t, par_set = sem("consts"), sem("const_v"), sem("par_t"), sem("par_set")
    x_sq, x_var, x_rstd, x_norm, x_t, x_hi, x_lo = (sem(n) for n in (
        "x_sq", "x_var", "x_rstd", "x_norm", "x_t", "x_hi", "x_lo"))
    vf_set, tok_t, tok_ev = sem("vf_set"), sem("tok_t"), sem("tok_ev")
    of_set, otok_t, otok_ev = sem("of_set"), sem("otok_t"), sem("otok_ev")
    gw_hi, gw_lo, g_mm, g_dve, g_act_in, g_act = (sem(n) for n in (
        "gw_hi", "gw_lo", "g_mm", "g_dve", "g_act_in", "g_act"))
    g_rows, g_t, g_set, ws_t, ws_set, v_var, v_rstd, m_out = (sem(n) for n in (
        "g_rows", "g_t", "g_set", "ws_t", "ws_set", "v_var", "v_rstd", "m_out"))
    gb_in, pool_step = sem("gb_in"), sem("pool_step")
    vn_step, vn_ready, sp_mm, u_ev, sp_used, z_ev, yg_ready, yg_hi, vr_out, yg_step, yg_lo = (sem(n) for n in (
        "vn_step", "vn_ready", "sp_mm", "u_ev", "sp_used", "z_ev", "yg_ready", "yg_hi", "vr_out", "yg_step",
        "yg_lo"))
    ma_sum, ma_hi, ma_lo = sem("ma_sum"), sem("ma_hi"), sem("ma_lo")
    h_const = sem("h_const")
    hst_in, c_in, n_in = sem("hst_in"), [sem("c_in0"), sem("c_in1")], sem("n_in")
    hist_t, hist_set, bc_row, bc_mm, w_arg, w_exp = (sem(n) for n in (
        "hist_t", "hist_set", "bc_row", "bc_mm", "w_arg", "w_exp"))
    q_ev, k_ev, v_ev, conv_step, silu_q, silu_k, qm_set = (sem(n) for n in (
        "q_ev", "k_ev", "v_ev", "conv_step", "silu_q", "silu_k", "qm_set"))
    ct_t, ct_ev, ct_n, s_mm, p_set, cn_set, cn_t, cst_ev = (sem(n) for n in (
        "ct_t", "ct_ev", "ct_n", "s_mm", "p_set", "cn_set", "cn_t", "cst_ev"))
    kt_t, kt_ev, kvs_t, kvs_ev, vt_t, vt_ev, num_mm, den_step, r_set, sq_set, var_set, rs_set, f_set = (
        sem(n) for n in ("kt_t", "kt_ev", "kvs_t", "kvs_ev", "vt_t", "vt_ev", "num_mm", "den_step", "r_set",
                         "sq_set", "var_set", "rs_set", "f_set"))
    h_set, ht_t, o_ev, z_set, gate_set, yf_set, ya_hi, cp_mm, cp_ev, nn_mm, nn_ev, vm_set, cs_mm, cs_ev = (
        sem(n) for n in ("h_set", "ht_t", "o_ev", "z_set", "gate_set", "yf_set", "ya_hi", "cp_mm", "cp_ev",
                         "nn_mm", "nn_ev", "vm_set", "cs_mm", "cs_ev"))
    q_step, ct_lo, lo_rows = sem("q_step"), sem("ct_lo"), sem("lo_rows")
    inter_mm = sem("inter_mm")
    ya_lo, st_mm, st_hi, st_lo = sem("ya_lo"), sem("st_mm"), sem("st_hi"), sem("st_lo")
    cst_out, cp_out, nn_out, cs_out = sem("cst_out"), sem("cp_out"), sem("nn_out"), [sem("cs_out0"), sem("cs_out1")]
    x_again, o_var, o_rstd, y_step, y_set, y_out = (sem(n) for n in (
        "x_again", "o_var", "o_rstd", "y_step", "y_set", "y_out"))

    def chunked(w):
        return w.rearrange("(c k p) n -> c p k n", k=CK, p=P)

    w_in_v, w_pa_v, w_pb_v, w_out_v = (chunked(w) for w in (w_in, w_pa, w_pb, w_out))
    xp_v = x_prompt.rearrange("o (n p) d -> p (o n) d", p=P)
    xs_v = x_sample.rearrange("b t d -> (b t) d")
    Cs_in = state_C.rearrange("b h (p v) k -> p b h (v k)", p=P)
    Cs_out = C_s.rearrange("b h (p v) k -> p b h (v k)", p=P)
    Cp_out = C_p.rearrange("o h (p v) k -> p (o h) (v k)", p=P)
    conv_in_v = state_conv.rearrange("b r (s n) -> (b r) s n", s=2)
    conv_p_v = conv_p.rearrange("o r (s n) -> (o r) s n", s=2)
    conv_s_v = conv_s.rearrange("b r (s n) -> (b r) s n", s=2)

    block = nc.Block()
    block.__enter__()

    def turned(b):
        return ps[:, 6 + b % 2, :].rearrange("p (k v q) -> p k v q", k=2, v=2)

    def key_major(t):
        return t[:, :, 0:DH].rearrange("p k (q v) -> p k v q", v=2)

    @block.sync
    def _(sp):
        sp.dma_start(xt[:, 0:2, :], xp_v).then_inc(x_in, 16)
        sp.dma_start(xt[0:S, 2, :], xs_v).then_inc(x_in, 16)
        sp.dma_start(prow[:, 0, :], w_conv.rearrange("j (n p) -> (j n) p", p=P)).then_inc(par_in, 16)
        sp.dma_start(prow[0:32, 1, :], b_conv.rearrange("(n p) -> n p", p=P)).then_inc(par_in, 16)
        sp.dma_start(prow[32:48, 1, :], g_pre.rearrange("(n p) -> n p", p=P)).then_inc(par_in, 16)
        sp.dma_start(prow[48:64, 1, :], g_head.rearrange("h (n p) -> (h n) p", p=P)).then_inc(par_in, 16)

        def load_pair(pair, w, col, first=False):
            for c in range(CHUNKS):
                if not first:
                    sp.wait_ge(lo_ready, 4 * pair - 3 + c)
                    sp.nop(nofuse=True)
                sp.dma_start(raw[:, c], w[c, :, :, ds(col, PW)]).then_inc(raw_landed[c], 16)

        load_pair(V0, w_in_v, COL_VB, first=True)
        with sp.Fori(1, 8) as i:
            load_pair(V0 + i, w_in_v, COL_VB + PW * i)
        with sp.Fori(0, GROUPS) as i:
            load_pair(G0 + 2 * i, w_in_v, COL_U + PW * i)
            load_pair(G0 + 1 + 2 * i, w_in_v, COL_ZB + PW * i)
        with sp.Fori(0, 8) as i:
            load_pair(MB0 + 2 * i, w_in_v, COL_GB + PW * i)
            load_pair(MB0 + 1 + 2 * i, w_pb_v, PW * i)
        with sp.Fori(0, HEADS) as h:
            for j, col in enumerate((COL_Q, COL_K, COL_V, COL_O, COL_ZA)):
                load_pair(H0 + j + 5 * h, w_in_v, col + PW * h)
        with sp.Fori(0, 8) as i:
            load_pair(MA0 + 2 * i, w_in_v, COL_GA + PW * i)
            load_pair(MA0 + 1 + 2 * i, w_pa_v, PW * i)
        with sp.Fori(0, 8) as i:
            load_pair(O0 + i, w_out_v, PW * i)
        sp.wait_ge(chunk_done, 4 * O0)
        sp.dma_start(xres[:, 0:2, :], xp_v).then_inc(x_again, 16)
        sp.dma_start(xres[0:S, 2, :], xs_v).then_inc(x_again, 16)
        sp.dma_start(gpost[:], g_post.partition_broadcast(P)).then_inc(x_again, 16)
        for t, out in enumerate((y_prompt[0, 0:P, :], y_prompt[0, P:TP, :], y_sample.rearrange("b t d -> (b t) d"))):
            sp.wait_ge(y_set, t + 1)
            n = P if t < 2 else S
            sp.dma_start(out, otok[0:n, t, :]).then_inc(y_out, 16)
        sp.wait_ge(y_out, 48)

    @block.tensor
    def _(pe):
        def chunk(pair, c, slot, free, mh_, ml_):
            pe.wait_ge(lo_ready, 4 * pair + (c + 1))
            if c == 0 and free is not None:
                pe.wait_ge(slot_free[slot], free)
            for kk in range(CK):
                k = CK * c + kk
                for j in range(2):
                    out = ps[:, 2 * slot + j, 0:T]
                    cols = slice(P * j, P * j + P)
                    nc.tensor.matmul(out, whi[:, c, kk, cols], mh_[:, k, :], start=(k == 0), stop=False)
                    nc.tensor.matmul(out, whi[:, c, kk, cols], ml_[:, k, :], start=False, stop=False)
                    last = nc.tensor.matmul(out, wlo[:, c, kk, cols], mh_[:, k, :], start=False,
                                            stop=(k == KT - 1))
            last.then_inc(chunk_done, 1)

        def turn(out_bank, src, j):
            for t in range(2):
                pe.transpose(ps[:, out_bank, PW * t + P * j:PW * t + P * j + P],
                             src[:, j, P * t:P * t + P], ident[:])
            return pe.transpose(ps[0:S, out_bank + 1, P * j:P * j + P], src[:, j, TP:T], ident[:])

        pe.wait_ge(par_in, 64)
        pe.wait_ge(consts, 1)
        pe.transpose(ps[:, 6, 0:P], prow[:, 0, :], ident[:])
        pe.transpose(ps[:, 6, P:P + 64], prow[0:64, 1, :], ident[0:64, 0:64]).then_inc(par_t, 1)
        pe.wait_ge(x_norm, 3)
        for k in range(KT):
            if k == 6:
                pe.wait_ge(par_set, 1)
            if k >= 8:
                pe.wait_ge(x_lo, k - 7)
            for t in range(2):
                pe.transpose(ps[:, k % 8, P * t:P * t + P], hb0[:, t, P * k:P * k + P], ident[:])
            pe.transpose(ps[:, k % 8, TP:T], hb0[0:S, 2, P * k:P * k + P],
                         ident[0:S, 0:S]).then_inc(x_t, 1)
        pe.wait_ge(x_lo, KT)

        def v_body(i, first=False):
            for s in range(2):
                for c in range(CHUNKS):
                    chunk(V0 + s + 2 * i, c, s, None if first else i, xh, xl)
            for s in range(2):
                pe.wait_ge(vf_set, 2 * i + s + 1)
                if not first:
                    pe.wait_ge(tok_ev, 2 * i + s - 1)
                turn(4 + 2 * s, vf[:, s], 0)
                turn(4 + 2 * s, vf[:, s], 1).then_inc(tok_t, 1)

        v_body(0, first=True)
        with pe.Fori(1, 4) as i:
            v_body(i)

        pe.wait_ge(gw_lo, 2)
        pe.wait_ge(tok_ev, 8)
        for k in range(KT):
            nc.tensor.matmul(ps[0:40, 4, 0:T], wgh[:, k, :], xh[:, k, :], start=(k == 0), stop=False)
            nc.tensor.matmul(ps[0:40, 4, 0:T], wgh[:, k, :], xl[:, k, :], start=False, stop=False)
            last = nc.tensor.matmul(ps[0:40, 4, 0:T], wgl[:, k, :], xh[:, k, :], start=False,
                                    stop=(k == KT - 1))
        last.then_inc(g_mm, 1)
        pe.wait_ge(w_sp_in, 32)
        for q in range(GROUPS):
            last = pe.transpose(ps[:, 6 + q // 4, P * (q % 4):P * (q % 4) + P], wsn[:, q, :], ident[:])
        last.then_inc(ws_t, 1)

        pe.wait_ge(ws_set, 2)
        nc.tensor.matmul(ps[0:S, 6, 0:S], rep4[:],
                         wsT[0:TS, :, 0:TS], start=True, stop=True).then_inc(ws_t, 1)

        def gates():
            pe.wait_ge(g_rows, 1)
            for t in range(2):
                pe.transpose(ps[:, 5, 96 * t:96 * t + 96], gqs[:, P * t:P * t + P], ident[0:96, 0:96])
            pe.transpose(ps[0:S, 5, 192:288], gqs[:, TP:T], ident[0:96, 0:96])
            nc.tensor.matmul(ps[:, 4, 0:64], ones8[:], gdx[:].rearrange("p a b -> p (a b)"),
                             start=True, stop=True)
            pe.transpose(ps[0:NB, 4, 64:72], gy[:, 2 * T + S:2 * T + S + NB], ident[0:8, 0:8])
            for j in range(2):
                last = pe.transpose(ps[:, 4, 128 + 64 * j:192 + 64 * j], nrow[:, P * j:P * j + P],
                                    ident[0:64, 0:64])
            last.then_inc(g_t, 1)

        def g_body(i, first=False):
            for c in range(CHUNKS):
                chunk(G0 + 2 * i, c, 0, G_USE[0] + i, xh, xl)
                if first and c == 1:
                    gates()
                if c == 2:
                    pe.wait_ge(vn_ready, i + 1)
                    if first:
                        pe.wait_ge(g_set, 1)
                        pe.wait_ge(ws_set, 3)
                    else:
                        pe.wait_ge(sp_used, i)
                    for j in range(2):
                        cols = slice(P * j, P * j + P)
                        nc.tensor.matmul(ps[:, 4 + j, 0:TP], onesrow[:],
                                         brow[0:1, ds(i, 1), :].broadcast_to([1, 2, P]), start=True, stop=False,
                                         skip_group_check=True)
                        nc.tensor.matmul(ps[:, 4 + j, TP:T], onesrow[:],
                                         brow[0:1, ds(i, 1), 0:TS].broadcast_to([1, NB, TS]), start=False,
                                         stop=False, skip_group_check=True)
                        for t in range(2):
                            nc.tensor.matmul(ps[:, 4 + j, P * t:P * t + P], vn[:, t, cols],
                                             wsT[:, ds(i, 1), :].squeeze(1), start=False, stop=True,
                                             skip_group_check=True)
                        last = nc.tensor.matmul(ps[:, 4 + j, TP:T], vn[0:S, 2, cols], wd[:, ds(i, 1), :].squeeze(1),
                                                start=False, stop=True, skip_group_check=True)
                    last.then_inc(sp_mm, 1)
            for c in range(CHUNKS):
                chunk(G0 + 1 + 2 * i, c, 1, G_USE[1] + i, xh, xl)

        g_body(0, first=True)
        with pe.Fori(1, GROUPS) as i:
            g_body(i)

        with pe.Fori(0, 8) as i:
            for c in range(CHUNKS):
                chunk(MB0 + 2 * i, c, 0, MB_USE[0] + i, xh, xl)
            pe.wait_ge(yg_lo, GROUPS)
            for c in range(CHUNKS):
                chunk(MB0 + 1 + 2 * i, c, 1, MB_USE[1] + i, yh, yl)

        X4, X5, X6, X7 = 4, 5, 6, 7

        def c_turn(h, b):
            if b % 4 == 0:
                pe.wait_ge(c_in[b // 4], 16 * h + 16)
            if b >= 2:
                pe.wait_ge(ct_lo, 8 * h + b - 1)
            for kh in range(2):
                for vh in range(2):
                    last = pe.transpose(ps[:, X6 + b % 2, DH * kh + P * vh:DH * kh + P * vh + P],
                                        Cin[:, b, vh, P * kh:P * kh + P], ident[:])
            last.then_inc(ct_t, 1)

        def inter(h, b):
            pe.wait_ge(ct_lo, 8 * h + b + 1)
            if b == 0:
                pe.wait_ge(qm_set, h + 1)
            for kh in range(2):
                for part_ in (CTh, CTl):
                    last = nc.tensor.matmul(ps[0:2 * S, X4, 0:DH + 2], qm[:, kh, 2 * S * b:2 * S * b + 2 * S], part_[:, kh, :],
                                            start=(b == 0 and kh == 0 and part_ is CTh), stop=(b == NB - 1 and kh == 1 and part_ is CTl),
                                            skip_group_check=True)
            last.then_inc(inter_mm, 1)

        def new_state(h, b):
            pe.wait_ge(vm_set, 8 * h + b + 1)
            if b >= 3:
                pe.wait_ge(cs_ev, 8 * h + b - 2)
            for vh in range(2):
                last = nc.tensor.matmul(ps[:, NEW_BANK[b % 3], DH * vh:DH * vh + DH],
                                        vm[:, b % 4, vh::2], kst[:], start=True, stop=True)
            last.then_inc(cs_mm, 1)

        with pe.Fori(0, HEADS) as h:
            for c in range(CHUNKS):
                chunk(H0 + 5 * h, c, 0, H_USE[0] + 3 * h, xh, xl)
                if c == 1:
                    pe.wait_ge(hst_in, 16 * h + 16)
                    pe.wait_ge(bc_row, h + 1)
                    pe.nop(nofuse=True)
                    for b in range(4):
                        last = pe.transpose(ps[:, X4, 24 * b:24 * b + 24],
                                            hst[:, b // 2, P * (b % 2):P * (b % 2) + P], ident[0:24, 0:24])
                    last.then_inc(hist_t, 1)
                if c == 2:
                    pe.wait_ge(hi_ready, 4 * (H0 + 1) + 1 + 20 * h)
                    nc.tensor.matmul(ps[:, X5, 0:T + S], ones8h[:], bcrow[:], start=True, stop=True
                                     ).then_inc(bc_mm, 1)
            for c in range(CHUNKS):
                chunk(H0 + 1 + 5 * h, c, 1, H_USE[1] + 2 * h, xh, xl)
            pe.wait_ge(hist_set, h + 1)
            for c in range(CHUNKS):
                chunk(H0 + 2 + 5 * h, c, 0, H_USE[0] + 1 + 3 * h, xh, xl)
                if c >= 1:
                    inter(h, c - 1)
                c_turn(h, c)
            for c in range(CHUNKS):
                chunk(H0 + 3 + 5 * h, c, 1, H_USE[1] + 1 + 2 * h, xh, xl)
                if c == 0:
                    pe.wait_ge(silu_k, 3 * h + 3)
                    pe.wait_ge(w_arg, h + 1)
                    for (lo, n, t0, at) in ((0, P, 0, 0), (P, P, P, TP), (TP, S, TP, 384)):
                        t1 = TP if lo < TP else T
                        for j in range(2):
                            last = nc.tensor.matmul(ps[0:n, X5, at:at + t1 - t0], qk[:, 2 + j, lo:lo + n],
                                                    qk[:, j, t0:t1], start=(j == 0), stop=(j == 1))
                    last.then_inc(s_mm, 1)
                if c == 1:
                    pe.wait_ge(cn_set, h + 1)
                    pe.wait_ge(p_set, h + 1)
                    for b in range(4):
                        last = pe.transpose(ps[0:27, X5, P * b:P * b + P], cn[:, b, :], ident[:])
                    last.then_inc(cn_t, 1)
                if c == 2:
                    pe.wait_ge(cst_ev, h + 1)
                    for j in range(2):
                        for t in range(2):
                            last = pe.transpose(ps[:, X5, DH * t + P * j:DH * t + P * j + P],
                                                qk[:, 2 + j, P * t:P * t + P], ident[:])
                    last.then_inc(kt_t, 1)
                if c == 3:
                    pe.wait_ge(kt_ev, h + 1)
                    pe.wait_ge(v_ev, h + 1)
                    for j in range(2):
                        pe.transpose(ps[0:S, X5, P * j:P * j + P], qk[:, 2 + j, TP:T], ident[:])
                        last = pe.transpose(ps[0:S, X5, DH + P * j:DH + P * j + P], vz[:, j, TP:T], ident[:])
                    last.then_inc(kvs_t, 1)
                inter(h, 3 + c)
                c_turn(h, 4 + c)
            for c in range(CHUNKS):
                chunk(H0 + 4 + 5 * h, c, 0, H_USE[0] + 2 + 3 * h, xh, xl)
                if c == 0:
                    inter(h, 7)
                    pe.wait_ge(kvs_ev, h + 1)
                    for j in range(2):
                        for t in range(2):
                            last = pe.transpose(ps[:, X5, DH * t + P * j:DH * t + P * j + P],
                                                vz[:, j, P * t:P * t + P], ident[:])
                    last.then_inc(vt_t, 1)
                    pe.wait_ge(slot_free[1], H_USE[1] + 2 + 2 * h)
                    nc.tensor.matmul(ps[:, 2, 0:DH], rep32[:], ktok[0:S, 2, :], start=True, stop=True)
                    nc.tensor.matmul(ps[:, 2, DH:2 * DH], rep32[:], vtok_h[0:S, 2, 0:DH], start=True,
                                     stop=True).then_inc(st_mm, 1)
                if c == 1:
                    pe.wait_ge(lo_rows, h + 1)
                    pe.wait_ge(vt_ev, h + 1)
                    nc.tensor.matmul(ps[:, X6, 0:DH + 1], W[:, 0:P], vtok_h[:, 0, :], start=True, stop=True)
                    nc.tensor.matmul(ps[:, X7, 0:DH + 1], W[:, P:TP], vtok_h[:, 0, :], start=True, stop=False)
                    nc.tensor.matmul(ps[:, X7, 0:DH + 1], W[:, TP:TP + P], vtok_h[:, 1, :], start=False,
                                     stop=True)
                    nc.tensor.matmul(ps[0:S, X4, 0:DH + 1], W[0:2 * S, 384:416], vtok_h[0:2 * S, 2, :],
                                     start=False, stop=True, skip_group_check=True).then_inc(num_mm, 1)
                    for b in range(3):
                        new_state(h, b)
                if c == 2:
                    for b in range(3, 6):
                        new_state(h, b)
                if c == 3:
                    pe.wait_ge(h_set, h + 1)
                    for j in range(2):
                        for t in range(2):
                            pe.transpose(ps[:, X6 + j, P * t:P * t + P], hb[:, t, P * j:P * j + P], ident[:])
                        last = pe.transpose(ps[:, X6 + j, TP:T], hb[0:S, 2, P * j:P * j + P],
                                            ident[0:S, 0:S])
                    last.then_inc(ht_t, 1)
                    nc.tensor.matmul(ps[0:NB, X4, 0:DH], mask8[0:S, :], ktok[0:S, 2, :], start=True, stop=True)
                    for t in range(2):
                        last = nc.tensor.matmul(ps[0:1, X4, DH:2 * DH], vtok_h[:, t, DH:DH + 1], ktok[:, t, :],
                                                start=(t == 0), stop=(t == 1))
                    last.then_inc(nn_mm, 1)
                    for b in range(6, NB):
                        new_state(h, b)
                    pe.wait_ge(cs_ev, 8 * h + 6)
                    for vh in range(2):
                        for t in range(2):
                            last = nc.tensor.matmul(ps[:, X5, DH * vh:DH * vh + DH], vtok_h[:, t, vh:DH:2],
                                                    ktok[:, t, :], start=(t == 0), stop=(t == 1))
                    last.then_inc(cp_mm, 1)

        pe.wait_ge(cs_ev, 8 * HEADS)
        with pe.Fori(0, 8) as i:
            for c in range(CHUNKS):
                chunk(MA0 + 2 * i, c, 0, MA_USE[0] + i, xh, xl)
            pe.wait_ge(ya_lo, HEADS)
            for c in range(CHUNKS):
                chunk(MA0 + 1 + 2 * i, c, 1, MA_USE[1] + i, yh, yl)

        def o_body(i, first=False):
            for s in range(2):
                for c in range(CHUNKS):
                    if first and s == 0:
                        pe.wait_ge(ma_lo, 2 * c + 2)
                    chunk(O0 + s + 2 * i, c, s, O_USE[s] + i, mh, ml)
            for s in range(2):
                pe.wait_ge(of_set, 2 * i + s + 1)
                if not first:
                    pe.wait_ge(otok_ev, 2 * i + s - 1)
                turn(4 + 2 * s, vf_o[:, s], 0)
                turn(4 + 2 * s, vf_o[:, s], 1).then_inc(otok_t, 1)

        o_body(0, first=True)
        with pe.Fori(1, 4) as i:
            o_body(i)

    @block.scalar
    def _(act):
        def split_hi(pair, c, first=False):
            act.wait_ge(raw_landed[c], 16 * pair + 16)
            if not first:
                act.wait_ge(chunk_done, 4 * pair - 3 + c)
            nc.scalar.activation(whi[:, c], raw[:, c], ACT.Copy).then_inc(hi_ready, 1)

        def results(slot):
            return ps[:, 2 * slot:2 * slot + 2, 0:T]

        act.wait_ge(x_in, 32)
        act.wait_ge(const_v, 1)
        for t in range(3):
            n = P if t < 2 else S
            nc.scalar.activation(hb0[0:n, t, :], xt[0:n, t, :], ACT.Square,
                                 accum_out=stat[0:n, t:t + 1]).then_inc(x_sq, 1)
        for c in range(CHUNKS):
            split_hi(0, c, first=True)
        act.wait_ge(par_set, 1)
        for k in range(KT):
            act.wait_ge(x_t, k + 1)
            nc.scalar.activation(xh[:, k, :], ps[:, k % 8, 0:T], ACT.Identity,
                                 scale=par1[:, 32 + k:33 + k]).then_inc(x_hi, 1)
        act.wait_ge(gin, 16)
        act.wait_ge(consts, 2)
        nc.scalar.activation(wgh[:, :, 0:8], wg[:, :, 0:8], ACT.Copy).then_inc(gw_hi, 1)
        nc.scalar.activation(wgh[:, :, 32:40], wg[:, :, 8:16], ACT.Copy).then_inc(gw_hi, 1)

        def v_body(i, first=False):
            for s in range(2):
                pair = V0 + s + 2 * i
                for c in range(CHUNKS):
                    split_hi(pair + 1, c)
                if not first:
                    act.wait_ge(tok_t, 2 * i + s - 1)
                nc.scalar.activation(vf[:, s], results(s), ACT.Copy).then_inc(vf_set, 1)
                act.wait_ge(vf_set, 2 * i + s + 1)
                act.sem_inc(slot_free[s], 1)

        v_body(0, first=True)
        with act.Fori(1, 4) as i:
            v_body(i)

        def gates():
            act.wait_ge(g_act_in, 1)
            nc.scalar.activation(gln[:], gab[:], ACT.Exp, scale=-1.0).then_inc(g_act, 1)
            act.wait_ge(g_act, 1)
            nc.scalar.activation(gln[:], gln[:], ACT.Ln, bias=1.0).then_inc(g_act, 1)
            act.wait_ge(g_act_in, 2)
            nc.scalar.activation(gy[:], gx[:], ACT.Exp).then_inc(g_act, 1)

        def g_body(i, first=False):
            for c in range(CHUNKS):
                split_hi(G0 + 1 + 2 * i, c)
                if first and c == 0:
                    gates()
            if not first:
                act.wait_ge(sp_used, i)
            nc.scalar.activation(uf[:], results(0), ACT.Copy).then_inc(slot_free[0], 1)
            for c in range(CHUNKS):
                split_hi(G0 + 2 + 2 * i, c)
            nc.scalar.activation(zs_g[:], results(1), ACT.Silu).then_inc(slot_free[1], 1)
            act.wait_ge(yg_ready, i + 1)
            nc.scalar.activation(yh[:, ds(2 * i, 2), :], yf_g[:], ACT.Copy).then_inc(yg_hi, 1)

        g_body(0, first=True)
        with act.Fori(1, GROUPS) as i:
            g_body(i)

        with act.Fori(0, 8) as i:
            for c in range(CHUNKS):
                split_hi(MB0 + 1 + 2 * i, c)
            act.wait_ge(slot_free[1], MB_USE[1] + i)
            nc.scalar.activation(tg[:], results(0), ACT.Tanh, scale=0.5).then_inc(slot_free[0], 1)
            for c in range(CHUNKS):
                split_hi(MB0 + 2 + 2 * i, c)

        def to_padded(j, slot, done):
            nc.scalar.activation(xp[:, j:j + 2, HIST:XPS], ps[:, 2 * slot:2 * slot + 2, 0:TP],
                                 ACT.Copy).then_inc(done, 1)
            for jj in range(2):
                last = nc.scalar.activation(
                    xp[:, j + jj, XPS:XPW].rearrange("p (b t) -> p b t", t=HIST + TS)[:, :, HIST:],
                    ps[:, 2 * slot + jj, TP:T].rearrange("p (b t) -> p b t", t=TS), ACT.Copy)
                last.then_inc(done, 1)

        def silu(j, done):
            nc.scalar.activation(qk[:, j:j + 2, 0:TP], acc[:, :, 0:TP], ACT.Silu).then_inc(done, 1)
            for jj in range(2):
                nc.scalar.activation(
                    qk[:, j + jj, TP:T].rearrange("p (b t) -> p b t", t=TS),
                    acc[:, jj, XPS:XPW].rearrange("p (b t) -> p b t", t=HIST + TS)[:, :, 0:TS],
                    ACT.Silu).then_inc(done, 1)

        def ct_copy(h, b):
            act.wait_ge(ct_t, 8 * h + b + 1)
            nc.scalar.activation(key_major(CTh), turned(b), ACT.Copy).then_inc(ct_ev, 1)

        with act.Fori(0, HEADS) as h:
            for c in range(CHUNKS):
                split_hi(H0 + 1 + 5 * h, c)
                if c == 3:
                    act.wait_ge(w_arg, h + 1)
                    nc.scalar.activation(W[:], W[:], ACT.Exp).then_inc(w_exp, 1)
            act.wait_ge(h_const, 1)
            to_padded(0, 0, q_ev)
            act.wait_ge(q_ev, 3 * h + 3)
            act.sem_inc(slot_free[0], 1)
            for c in range(CHUNKS):
                split_hi(H0 + 2 + 5 * h, c)
                if c == 2:
                    act.wait_ge(conv_step, 16 * h + 8)
                    silu(0, silu_q)
            to_padded(2, 1, k_ev)
            act.wait_ge(k_ev, 3 * h + 3)
            act.sem_inc(slot_free[1], 1)
            for c in range(CHUNKS):
                split_hi(H0 + 3 + 5 * h, c)
                ct_copy(h, c)
                if c == 2:
                    act.wait_ge(conv_step, 16 * h + 16)
                    silu(2, silu_k)
            nc.scalar.activation(vz[:], results(0), ACT.Copy).then_inc(v_ev, 1)
            act.wait_ge(v_ev, h + 1)
            act.sem_inc(slot_free[0], 1)
            for c in range(CHUNKS):
                split_hi(H0 + 4 + 5 * h, c)
                ct_copy(h, 4 + c)
                if c == 2:
                    act.wait_ge(kt_t, h + 1)
                    nc.scalar.activation(ktok[:, 0, :], ps[:, 5, 0:DH], ACT.Identity,
                                         scale=gq[:, 0, ds(h + 64, 1)])
                    nc.scalar.activation(ktok[:, 1, :], ps[:, 5, DH:2 * DH], ACT.Identity,
                                         scale=gq[:, 1, ds(h + 64, 1)]).then_inc(kt_ev, 1)
                if c == 3:
                    act.wait_ge(kvs_t, h + 1)
                    nc.scalar.activation(ktok[0:S, 2, :], ps[0:S, 5, 0:DH], ACT.Identity,
                                         scale=gq[0:S, 2, ds(h + 64, 1)])
                    nc.scalar.activation(vtok_h[0:S, 2, 0:DH], ps[0:S, 5, DH:2 * DH],
                                         ACT.Copy).then_inc(kvs_ev, 1)
            nc.scalar.activation(og[:], results(1), ACT.Tanh, scale=0.5).then_inc(slot_free[1], 1)
            for c in range(CHUNKS):
                split_hi(H0 + 5 + 5 * h, c)
                if c == 0:
                    act.wait_ge(vt_t, h + 1)
                    nc.scalar.activation(vtok_h[:, 0:2, 0:DH], ps[:, 5, :].rearrange("p (t v) -> p t v", t=2),
                                         ACT.Copy).then_inc(vt_ev, 1)
                    act.wait_ge(inter_mm, 8 * h + 8)
                    nc.scalar.activation(vtok_h[S:2 * S, 2, :], ps[S:2 * S, 4, 0:DH + 1],
                                         ACT.Copy).then_inc(lo_rows, 1)
                    act.wait_ge(st_mm, h + 1)
                    nc.scalar.activation(kst[:], ps[:, 2, 0:DH], ACT.Copy)
                    nc.scalar.activation(vst[:], ps[:, 2, DH:2 * DH], ACT.Copy).then_inc(st_hi, 1)
                if c == 1:
                    act.wait_ge(r_set, h + 1)
                    for t, (n, bank) in enumerate(((P, 6), (P, 7), (S, 4))):
                        nc.scalar.activation(hb[0:n, t, :], ps[0:n, bank, 0:DH], ACT.Square,
                                             scale=r3[0:n, t:t + 1],
                                             accum_out=q3[0:n, t:t + 1]).then_inc(sq_set, 1)
                if c == 2:
                    act.wait_ge(f_set, h + 1)
                    act.wait_ge(sq_set, 3 * h + 3)
                    for t, (n, bank) in enumerate(((P, 6), (P, 7), (S, 4))):
                        last = nc.scalar.activation(hb[0:n, t, :], ps[0:n, bank, 0:DH], ACT.Identity,
                                                    scale=f3[0:n, t:t + 1])
                    last.then_inc(h_set, 1)
            nc.scalar.activation(vz[:], results(0), ACT.Silu).then_inc(z_set, 1)
            act.wait_ge(z_set, h + 1)
            act.sem_inc(slot_free[0], 1)
            act.wait_ge(yf_set, h + 1)
            nc.scalar.activation(yh[:, ds(2 * h, 2), :], yf[:], ACT.Copy).then_inc(ya_hi, 1)
            act.wait_ge(cp_mm, h + 1)
            nc.scalar.activation(cpo[:], ps[:, 5, :].rearrange("p (v k) -> p v k", v=2),
                                 ACT.Copy).then_inc(cp_ev, 1)
            act.wait_ge(cp_ev, h + 1)

        with act.Fori(0, 8) as i:
            for c in range(CHUNKS):
                split_hi(MA0 + 1 + 2 * i, c)
            act.wait_ge(slot_free[1], MA_USE[1] + i)
            nc.scalar.activation(tg[:], results(0), ACT.Tanh, scale=0.5).then_inc(slot_free[0], 1)
            for c in range(CHUNKS):
                split_hi(MA0 + 2 + 2 * i, c)
            act.wait_ge(ma_sum, i + 1)
            nc.scalar.activation(mh[:, ds(2 * i, 2), :], sm[:], ACT.Copy, scale=0.5).then_inc(ma_hi, 1)

        def o_body(i, first=False, last=False):
            for s in range(2):
                if not (last and s == 1):
                    for c in range(CHUNKS):
                        split_hi(O0 + 1 + s + 2 * i, c)
                if last and s == 1:
                    act.wait_ge(chunk_done, 4 * PAIRS)
                if not first:
                    act.wait_ge(otok_t, 2 * i + s - 1)
                nc.scalar.activation(vf_o[:, s], results(s), ACT.Copy).then_inc(of_set, 1)
                act.wait_ge(of_set, 2 * i + s + 1)
                act.sem_inc(slot_free[s], 1)

        o_body(0, first=True)
        with act.Fori(1, 3) as i:
            o_body(i)
        o_body(3, last=True)

    @block.vector
    def _(dve):
        def split_lo(pair, c):
            dve.wait_ge(hi_ready, 4 * pair + c + 1)
            nc.vector.tensor_tensor(wlo[:, c], raw[:, c], whi[:, c].bitcast(F32),
                                    ALU.subtract).then_inc(lo_ready, 1)

        def bc(ap, axis, shape):
            return ap.unsqueeze(axis).broadcast_to(shape)

        nc.vector.memset(stat[:], 1.0).then_inc(const_v, 1)
        dve.wait_ge(par_t, 1)
        nc.vector.tensor_copy(par0[:], ps[:, 6, 0:P])
        nc.vector.tensor_copy(par1[:], ps[:, 6, P:P + 64])
        nc.vector.tensor_scalar(ghh[:], ps[:, 6, P + 48:P + 64], 0.5, None, ALU.mult).then_inc(par_set, 1)
        dve.wait_ge(x_sq, 3)
        nc.vector.tensor_scalar(stat[:], stat[:], 1.0 / D, EPS, ALU.mult, ALU.add).then_inc(x_var, 1)
        dve.wait_ge(x_rstd, 1)
        for t in range(3):
            n = P if t < 2 else S
            nc.vector.tensor_scalar(hb0[0:n, t, :], xt[0:n, t, :], rstd[0:n, t:t + 1], None,
                                    ALU.mult).then_inc(x_norm, 1)
        for c in range(CHUNKS):
            split_lo(0, c)
        dve.wait_ge(par_set, 1)
        for k in range(KT):
            dve.wait_ge(x_hi, k + 1)
            nc.vector.scalar_tensor_tensor(xl[:, k, :], ps[:, k % 8, 0:T], par1[:, 32 + k:33 + k],
                                           xh[:, k, :].bitcast(F32), ALU.mult, ALU.subtract).then_inc(x_lo, 1)
        dve.wait_ge(gw_hi, 2)
        for j in range(2):
            nc.vector.tensor_tensor(wgl[:, :, 32 * j:32 * j + 8], wg[:, :, 8 * j:8 * j + 8],
                                    wgh[:, :, 32 * j:32 * j + 8].bitcast(F32),
                                    ALU.subtract).then_inc(gw_lo, 1)
        nc.vector.memset(mv[:], 1.0).then_inc(v_var, 1)

        def v_body(i):
            for s in range(2):
                for c in range(CHUNKS):
                    split_lo(V0 + 1 + s + 2 * i, c)
            for s in range(2):
                dve.wait_ge(tok_t, 2 * i + s + 1)
                b = 4 + 2 * s
                col = 2 * PW * i + PW * s
                for t in range(2):
                    nc.vector.bn_stats(vstat[:, t, ds(2 * i + s, 1), :], ps[:, b, PW * t:PW * t + PW])
                nc.vector.bn_stats(vstat[0:S, 2, ds(2 * i + s, 1), :], ps[0:S, b + 1, 0:PW])
                nc.vector.tensor_copy(vtok[:, 0:2, ds(col, PW)], ps[:, b, :].rearrange("p (t v) -> p t v", t=2))
                nc.vector.tensor_copy(vtok[0:S, 2, ds(col, PW)], ps[0:S, b + 1, 0:PW]).then_inc(tok_ev, 1)

        with dve.Fori(0, 4) as i:
            v_body(i)
        dve.wait_ge(tok_ev, 8)
        dve.wait_ge(v_var, 1)
        for t in range(3):
            n = P if t < 2 else S
            nc.vector.bn_aggr(mv[0:n, t, :], vstat[0:n, t].rearrange("p a b -> p (a b)")).then_inc(v_var, 1)
        dve.wait_ge(v_var, 4)
        nc.vector.tensor_scalar(stat[:], mv[:, :, 1:2].squeeze(2), EPS, None, ALU.add).then_inc(v_var, 1)
        nc.vector.tensor_scalar(nmu[:], mv[:, :, 0:1].squeeze(2), -1.0, None, ALU.mult).then_inc(v_var, 1)
        dve.wait_ge(ws_t, 1)
        dve.wait_ge(consts, 2)
        nc.vector.tensor_copy(rep4[:].rearrange("p (b t) -> p b t", t=TS),
                              bc(ident[0:TS, 0:TS], 1, [TS, NB, TS]))
        for q in range(2):
            nc.vector.tensor_tensor(wsT[:, 4 * q:4 * q + 4, :], ps[:, 6 + q, :].rearrange("p (g t) -> p g t", g=4),
                                    bc(tri01[:], 1, [P, 4, P]), ALU.mult).then_inc(ws_set, 1)
        dve.wait_ge(ws_t, 2)
        nc.vector.tensor_tensor(wd[:].rearrange("p g (b t) -> p g b t", t=TS),
                                bc(ps[0:S, 6, 0:S].rearrange("p (g t) -> p g t", t=TS), 2, [S, GROUPS, NB, TS]),
                                bc(blk01[:].rearrange("p (b t) -> p b t", t=TS), 1, [S, GROUPS, NB, TS]),
                                ALU.mult).then_inc(ws_set, 1)

        step = Steps(dve, g_dve)
        smp = lambda t: t[:, TP:T].rearrange("p (b t) -> p b t", t=TS)

        def gates_a():
            dve.wait_ge(g_mm, 1)
            step(nc.vector.tensor_copy(gf[:], ps[32:40, 4, 0:T]))
            step(nc.vector.tensor_scalar(gf[:], gf[:], bg[:, 1:2], None, ALU.add))
            nc.vector.scalar_tensor_tensor(gab[:], gf[:], -1.0, gf[:], ALU.mult, ALU.max).then_inc(g_act_in, 1)

        def gates_b():
            dve.wait_ge(g_act, 2)
            step(nc.vector.scalar_tensor_tensor(glf[:], gf[:], 0.0, gln[:], ALU.min, ALU.subtract))
            step(nc.vector.tensor_tensor_scan(gbc[:], r01[:], glf[:], 0.0, ALU.mult, ALU.add))
            step(nc.vector.scalar_tensor_tensor(ga_[:], ps[0:8, 4, 0:T], bg[:, 0:1], gbc[:], ALU.add,
                                                ALU.subtract))
            step(nc.vector.tensor_copy(gd1[:], ga_[:]))
            step(nc.vector.tensor_scalar(gd1[:, 0:1], ga_[:, 0:1], 0.0, None, ALU.max))
            step(nc.vector.tensor_tensor(smp(gd1)[:, :, 0:1].squeeze(2), smp(ga_)[:, :, 0:1].squeeze(2), m0[:],
                                         ALU.max))
            step(nc.vector.tensor_tensor_scan(gM[:], rneg[:], gd1[:], 0.0, ALU.add, ALU.max))
            last = smp(gM)[:, :, TS - 1:TS]
            step(nc.vector.scalar_tensor_tensor(gx[:, 0:T], gM[:], -1.0, gbc[:], ALU.mult, ALU.subtract))
            step(nc.vector.tensor_scalar(gx[:, T:T + TP], ga_[:, 0:TP], gM[:, TP - 1:TP], None, ALU.subtract))
            step(nc.vector.tensor_tensor(gx[:, T + TP:2 * T].rearrange("p (b t) -> p b t", t=TS), smp(ga_),
                                         last.broadcast_to([HEADS, NB, TS]), ALU.subtract))
            step(nc.vector.tensor_tensor(gx[:, 2 * T:2 * T + S].rearrange("p (b t) -> p b t", t=TS),
                                         bc(m0[:], 2, [HEADS, NB, TS]), smp(gM), ALU.subtract))
            nc.vector.tensor_tensor(gx[:, 2 * T + S:], m0[:], last.squeeze(2), ALU.subtract
                                    ).then_inc(g_act_in, 1)
            nc.vector.tensor_scalar(nb[:, 0:T], gM[:], -1.0, None, ALU.mult)
            nc.vector.tensor_tensor(gmn[:, 0:1], gbc[:, TP - 1:TP], gM[:, TP - 1:TP], ALU.add)
            step(nc.vector.tensor_tensor(gmn[:, 1:], smp(gbc)[:, :, TS - 1:TS].squeeze(2), last.squeeze(2), ALU.add))

        def gates_c():
            dve.wait_ge(g_act, 3)
            nc.vector.tensor_copy(gqs[0:8, :], ga_[:])
            nc.vector.tensor_copy(gqs[32:40, :], gy[:, 0:T])
            nc.vector.tensor_scalar(gqs[64:72, :], gy[:, T:2 * T], DH ** -0.5, None, ALU.mult)
            nc.vector.tensor_copy(nb[:, T:], gy[:, 2 * T:2 * T + S])
            nc.vector.tensor_tensor(gdx[:], bc(gy[:, 2 * T + S:], 1, [HEADS, HEADS, NB]),
                                    bc(eye8[:], 2, [HEADS, HEADS, NB]), ALU.mult).then_inc(g_rows, 1)

        def gates_d():
            n_turned = ps[:, 4, 128:256].rearrange("p (k n) -> p k n", k=2)
            dve.wait_ge(g_t, 1)
            nc.vector.tensor_copy(gq[:, 0:2, :], ps[:, 5, 0:192].rearrange("p (t q) -> p t q", t=2))
            nc.vector.tensor_copy(gq[0:S, 2, :], ps[0:S, 5, 192:288])
            nc.vector.tensor_copy(dec_bc[:], ps[:, 4, 0:64])
            nc.vector.tensor_copy(decT[:], ps[0:NB, 4, 64:72])
            step(nc.vector.tensor_copy(nTh[:], n_turned))
            nc.vector.tensor_tensor(nTl[:], n_turned, nTh[:].bitcast(F32), ALU.subtract).then_inc(g_set, 1)

        def g_body(i, first=False):
            if not first:
                dve.wait_ge(sp_mm, i)
                dve.wait_ge(vr_out, 32 * i)
            else:
                dve.wait_ge(v_rstd, 1)
                dve.wait_ge(v_var, 6)
                dve.wait_ge(ln_in, 32)
            vstep = Steps(dve, vn_step, 2 * i)
            col = ds(DH * i, DH)
            for t in range(3):
                n = P if t < 2 else S
                ins = nc.vector.tensor_scalar(vn[0:n, t, :], vtok[0:n, t, col], nmu[0:n, t:t + 1],
                                              rstd[0:n, t:t + 1], ALU.add, ALU.mult)
            vstep(ins)
            nc.vector.tensor_tensor(vn[:, 0:2, :], vn[:, 0:2, :], bc(lng[:, col], 1, [P, 2, DH]), ALU.mult)
            vstep(nc.vector.tensor_tensor(vn[0:S, 2, :], vn[0:S, 2, :], lng[0:S, col], ALU.mult))
            nc.vector.tensor_tensor(vn[:, 0:2, :], vn[:, 0:2, :], bc(lnb[:, col], 1, [P, 2, DH]), ALU.add)
            nc.vector.tensor_tensor(vn[0:S, 2, :], vn[0:S, 2, :], lnb[0:S, col], ALU.add).then_inc(vn_ready, 1)
            for c in range(CHUNKS):
                split_lo(G0 + 1 + 2 * i, c)
                if first:
                    (gates_b, gates_c, gates_d, lambda: None)[c]()
            for c in range(CHUNKS):
                split_lo(G0 + 2 + 2 * i, c)
                if c == 0:
                    dve.wait_ge(sp_mm, i + 1)
                    dve.wait_ge(slot_free[0], G_USE[0] + i + 1)
                    nc.vector.tensor_tensor(tt_g[:], ps[:, 4:6, 0:T], uf[:], ALU.mult).then_inc(sp_used, 1)
            dve.wait_ge(slot_free[1], G_USE[1] + i + 1)
            dve.wait_ge(sp_used, i + 1)
            nc.vector.tensor_tensor(yf_g[:], tt_g[:], zs_g[:], ALU.mult).then_inc(yg_ready, 1)
            dve.wait_ge(yg_hi, i + 1)
            nc.vector.tensor_tensor(yl[:, ds(2 * i, 2), :], yf_g[:], yh[:, ds(2 * i, 2), :].bitcast(F32),
                                    ALU.subtract).then_inc(yg_lo, 1)

        gates_a()
        g_body(0, first=True)
        with dve.Fori(1, GROUPS) as i:
            g_body(i)

        with dve.Fori(0, 8) as i:
            for j in range(2):
                for c in range(CHUNKS):
                    split_lo(MB0 + 1 + j + 2 * i, c)
            dve.wait_ge(slot_free[0], MB_USE[0] + i + 1)
            dve.wait_ge(chunk_done, 4 * MB0 + 8 + 8 * i)
            nc.vector.scalar_tensor_tensor(part[:, ds(2 * i, 2), :], tg[:], 1.0, ps[:, 2:4, 0:T], ALU.add,
                                           ALU.mult).then_inc(slot_free[1], 1)

        dve.wait_ge(vr_out, 32 * GROUPS)
        nc.vector.memset(qm[:].bitcast(F32), 0.0)
        nc.vector.memset(CTh[:].bitcast(F32), 0.0)
        nc.vector.memset(CTl[:].bitcast(F32), 0.0)
        nc.vector.memset(xp[:, :, 0:HIST], 0.0)
        nc.vector.memset(vtok_h[:, :, DH:DH + 1], 1.0)
        nc.vector.memset(r3[:], 1.0)
        nc.vector.memset(q3[:], 1.0)
        nc.vector.memset(f3[:], 1.0)
        nc.vector.memset(W[:], 0.0)
        nc.vector.memset(ones8h[:], 1.0).then_inc(h_const, 1)
        dve.wait_ge(h_const, 1)

        def conv(h, j, blk, taps):
            for tap in taps:
                for jj in range(2):
                    w_at = par0[:, ds(2 * h + (32 * tap + blk + jj), 1)]
                    out, src = acc[:, jj, 0:CW], xp[:, j + jj, tap:tap + CW]
                    if tap == 0:
                        ins = nc.vector.tensor_scalar(out, src, w_at, par1[:, ds(2 * h + (blk + jj), 1)],
                                                      ALU.mult, ALU.add)
                    else:
                        dve.wait_ge(conv_step, 16 * h + (4 * j + 2 * tap + jj - 1))
                        ins = nc.vector.scalar_tensor_tensor(out, src, w_at, out, ALU.mult, ALU.add)
                    ins.then_inc(conv_step, 1)

        def own(part_):
            return qm[:, :, part_:part_ + NB * (2 * S + TS)].rearrange(
                "p k (b x) -> p k b x", x=2 * S + TS)[:, :, :, 0:TS]

        def ct_split(h, b):
            dve.wait_ge(ct_ev, 8 * h + b + 1)
            for t, n in ((CTh, nTh), (CTl, nTl)):
                nc.vector.tensor_copy(t[:, :, DH:DH + 1], n[:, :, ds(h + 8 * b, 1)].bitcast(F32))
            nc.vector.tensor_tensor(key_major(CTl), turned(b), key_major(CTh).bitcast(F32),
                                    ALU.subtract).then_inc(ct_lo, 1)

        def of_sequence(h, b):
            if b >= 4:
                dve.wait_ge(cs_mm, 8 * h + b - 3)
            nc.vector.tensor_scalar(vm[:, b % 4, :], vst[:].bitcast(F32), mask8[:, b:b + 1], None,
                                    ALU.mult).then_inc(vm_set, 1)

        def add_state(h, b):
            dve.wait_ge(cs_mm, 8 * h + b + 1)
            nc.vector.scalar_tensor_tensor(Cin[:, b], Cin[:, b], dec_bc[:, ds(8 * h + b, 1)],
                                           ps[:, NEW_BANK[b % 3], :].rearrange("p (v k) -> p v k", v=2),
                                           ALU.mult, ALU.add).then_inc(cs_ev, 1)

        with dve.Fori(0, HEADS) as h:
            nc.vector.tensor_scalar(bcrow[:], nb[:], eye8[:, ds(h, 1)], None, ALU.mult).then_inc(bc_row, 1)
            for c in range(CHUNKS):
                split_lo(H0 + 1 + 5 * h, c)
                if c == 1:
                    dve.wait_ge(hist_t, h + 1)
                    for j in range(4):
                        last = nc.vector.tensor_copy(
                            xp[:, j, XPS:XPW].rearrange("p (b t) -> p b t", t=HIST + TS)[:, :, 0:HIST],
                            ps[:, 4, 24 * j:24 * j + 24].rearrange("p (b t) -> p b t", t=HIST))
                    last.then_inc(hist_set, 1)
                if c == 2:
                    dve.wait_ge(bc_mm, h + 1)
                    nc.vector.tensor_copy(scb[:], bc(ps[:, 5, T:T + S], 1, [P, 2, S]))
                    nc.vector.tensor_scalar(W[:, P:TP], ps[:, 5, P:TP], gq[:, 0, ds(h, 1)], None, ALU.add)
                    for t, (lo, n, at, mask) in enumerate(((0, P, 0, 0), (P, P, TP, 0), (TP, S, 384, P))):
                        last = nc.vector.scalar_tensor_tensor(
                            W[:, at:at + n], ps[:, 5, lo:lo + n], gq[:, t, ds(h, 1)], keep_w[:, mask:mask + n],
                            ALU.add, ALU.min)
                    last.then_inc(w_arg, 1)
            for c in range(CHUNKS):
                split_lo(H0 + 2 + 5 * h, c)
                if c == 0:
                    dve.wait_ge(q_ev, 3 * h + 3)
                    dve.wait_ge(hist_set, h + 1)
                    conv(h, 0, 0, (0, 1))
                if c == 1:
                    conv(h, 0, 0, (2, 3))
                if c == 3:
                    dve.wait_ge(silu_q, 3 * h + 3)
                    qs = Steps(dve, q_step, 2 * h)
                    qs(nc.vector.tensor_tensor(scb[:], qk[:, 0:2, TP:T], scb[:], ALU.mult))
                    scaled = scb[:].rearrange("p k (b t) -> p k b t", t=TS)
                    qs(nc.vector.tensor_copy(own(0), scaled))
                    last = nc.vector.tensor_tensor(own(S), scaled, own(0).bitcast(F32), ALU.subtract)
                    last.then_inc(qm_set, 1)
            for c in range(CHUNKS):
                split_lo(H0 + 3 + 5 * h, c)
                ct_split(h, c)
                if c == 0:
                    dve.wait_ge(k_ev, 3 * h + 3)
                    conv(h, 2, 16, (0, 1))
                if c == 1:
                    conv(h, 2, 16, (2, 3))
                if c == 2:
                    nc.vector.tensor_copy(cn[:, :, 0:3], xp[:, :, TP:XPS])
                    for j in range(4):
                        last = nc.vector.tensor_copy(
                            cn[:, j, 3:27].rearrange("p (b t) -> p b t", t=3),
                            xp[:, j, XPS:XPW].rearrange("p (b t) -> p b t", t=HIST + TS)[:, :, TS:])
                    last.then_inc(cn_set, 1)
            for c in range(CHUNKS):
                split_lo(H0 + 4 + 5 * h, c)
                ct_split(h, 4 + c)
                if c == 0:
                    dve.wait_ge(s_mm, h + 1)
                    dve.wait_ge(w_exp, h + 1)
                    nc.vector.scalar_tensor_tensor(W[:, 0:384], ps[:, 5, 0:384], DH ** -0.5, W[:, 0:384],
                                                   ALU.mult, ALU.mult)
                    nc.vector.tensor_copy(W[S:2 * S, 384:416], ident[S:2 * S, S:2 * S])
                    nc.vector.scalar_tensor_tensor(W[0:S, 384:416], ps[0:S, 5, 384:416], DH ** -0.5,
                                                   W[0:S, 384:416], ALU.mult, ALU.mult).then_inc(p_set, 1)
                if c == 1:
                    dve.wait_ge(cn_t, h + 1)
                    nc.vector.tensor_copy(cst[:].rearrange("p a b -> p (a b)"), ps[0:27, 5, :]).then_inc(cst_ev, 1)
            for c in range(CHUNKS):
                split_lo(H0 + 5 + 5 * h, c)
                if c == 0:
                    dve.wait_ge(st_hi, h + 1)
                    for t, col, rows in ((kst, 0, slice(S, 2 * S)), (kst, 0, slice(3 * S, P)),
                                         (vst, DH, slice(2 * S, P))):
                        last = nc.vector.tensor_tensor(t[rows], ps[rows, 2, col:col + DH], t[rows].bitcast(F32),
                                                       ALU.subtract)
                    last.then_inc(st_lo, 1)
                    dve.wait_ge(st_lo, h + 1)
                    for b in range(4):
                        of_sequence(h, b)
                if c == 1:
                    dve.wait_ge(num_mm, h + 1)
                    for t, (n, bank) in enumerate(((P, 6), (P, 7), (S, 4))):
                        last = nc.vector.tensor_copy(f3[0:n, t:t + 1], ps[0:n, bank, DH:DH + 1])
                    den = Steps(dve, den_step, 3 * h)
                    den(last)
                    den(nc.vector.scalar_tensor_tensor(q3[:], f3[:], -1.0, f3[:], ALU.mult, ALU.max))
                    den(nc.vector.tensor_tensor(q3[:], q3[:], gq[:, :, ds(h + 32, 1)].squeeze(2), ALU.max))
                    nc.vector.reciprocal(r3[:], q3[:]).then_inc(r_set, 1)
                    add_state(h, 0)
                    of_sequence(h, 4)
                    add_state(h, 1)
                    of_sequence(h, 5)
                    dve.wait_ge(sq_set, 3 * h + 3)
                    nc.vector.tensor_scalar(stat[:], q3[:], 1.0 / DH, EPS, ALU.mult, ALU.add).then_inc(var_set, 1)
                    add_state(h, 2)
                    dve.wait_ge(rs_set, h + 1)
                    nc.vector.tensor_tensor(f3[:], r3[:], rstd[:], ALU.mult).then_inc(f_set, 1)
                if c == 2:
                    add_state(h, 3)
                    of_sequence(h, 6)
                    add_state(h, 4)
                    of_sequence(h, 7)
                    add_state(h, 5)
            dve.wait_ge(z_set, h + 1)
            dve.wait_ge(slot_free[1], H_USE[1] + 2 + 2 * h)
            nc.vector.scalar_tensor_tensor(og[:], og[:], 1.0, vz[:], ALU.add, ALU.mult).then_inc(gate_set, 1)
            dve.wait_ge(gate_set, h + 1)
            dve.wait_ge(ht_t, h + 1)
            for j in range(2):
                last = nc.vector.scalar_tensor_tensor(yf[:, j, :], ps[:, 6 + j, 0:T], ghh[:, ds(2 * h + j, 1)],
                                                      og[:, j, :], ALU.mult, ALU.mult)
            last.then_inc(yf_set, 1)
            dve.wait_ge(ya_hi, h + 1)
            nc.vector.tensor_tensor(yl[:, ds(2 * h, 2), :], yf[:], yh[:, ds(2 * h, 2), :].bitcast(F32),
                                    ALU.subtract).then_inc(ya_lo, 1)
            dve.wait_ge(nn_mm, h + 1)
            dve.wait_ge(n_in, 16 * h + 16)
            nc.vector.scalar_tensor_tensor(nout[:, 0, :], nin[:], decT[:, ds(h, 1)], ps[0:NB, 4, 0:DH],
                                           ALU.mult, ALU.add)
            nc.vector.tensor_copy(nout[0:1, 1, :], ps[0:1, 4, DH:2 * DH]).then_inc(nn_ev, 1)
            for b in range(6, NB):
                add_state(h, b)
            dve.wait_ge(nn_ev, h + 1)
            dve.wait_ge(cs_ev, 8 * h + 8)

        def left():
            for s, n in ((cs_out[0], 8), (cs_out[1], 8), (cp_out, 8), (nn_out, 16), (cst_out, 16)):
                dve.wait_ge(s, 16 * n)

        with dve.Fori(0, 8) as i:
            for j in range(2):
                for c in range(CHUNKS):
                    split_lo(MA0 + 1 + j + 2 * i, c)
            dve.wait_ge(slot_free[0], MA_USE[0] + i + 1)
            dve.wait_ge(chunk_done, 4 * MA0 + 8 + 8 * i)
            left()
            nc.vector.scalar_tensor_tensor(tm[:], tg[:], 1.0, ps[:, 2:4, 0:T], ALU.add,
                                           ALU.mult).then_inc(slot_free[1], 1)
            dve.wait_ge(slot_free[1], MA_USE[1] + i + 1)
            nc.vector.tensor_tensor(sm[:], tm[:], part[:, ds(2 * i, 2), :], ALU.add).then_inc(ma_sum, 1)
            dve.wait_ge(ma_hi, i + 1)
            nc.vector.scalar_tensor_tensor(ml[:, ds(2 * i, 2), :], sm[:], 0.5,
                                           mh[:, ds(2 * i, 2), :].bitcast(F32), ALU.mult,
                                           ALU.subtract).then_inc(ma_lo, 1)

        def o_body(i, last=False):
            for s in range(1 if last else 2):
                for c in range(CHUNKS):
                    split_lo(O0 + 1 + s + 2 * i, c)
            for s in range(2):
                dve.wait_ge(otok_t, 2 * i + s + 1)
                b = 4 + 2 * s
                col = 2 * PW * i + PW * s
                for t in range(2):
                    nc.vector.bn_stats(ostat[:, t, ds(2 * i + s, 1), :], ps[:, b, PW * t:PW * t + PW])
                nc.vector.bn_stats(ostat[0:S, 2, ds(2 * i + s, 1), :], ps[0:S, b + 1, 0:PW])
                nc.vector.tensor_copy(otok[:, 0:2, ds(col, PW)], ps[:, b, :].rearrange("p (t v) -> p t v", t=2))
                nc.vector.tensor_copy(otok[0:S, 2, ds(col, PW)], ps[0:S, b + 1, 0:PW]).then_inc(otok_ev, 1)

        nc.vector.memset(omv[:], 1.0).then_inc(o_var, 1)
        with dve.Fori(0, 3) as i:
            o_body(i)
        o_body(3, last=True)
        dve.wait_ge(otok_ev, 8)
        dve.wait_ge(o_var, 1)
        for t in range(3):
            n = P if t < 2 else S
            nc.vector.bn_aggr(omv[0:n, t, :], ostat[0:n, t].rearrange("p a b -> p (a b)")).then_inc(o_var, 1)
        dve.wait_ge(o_var, 4)
        mean, var = omv[:, :, 0:1].squeeze(2), omv[:, :, 1:2].squeeze(2)
        nc.vector.tensor_tensor(stat[:], mean, mean, ALU.mult).then_inc(o_var, 1)
        dve.wait_ge(o_var, 5)
        nc.vector.scalar_tensor_tensor(stat[:], stat[:], EPS, var, ALU.add, ALU.add).then_inc(o_var, 1)
        dve.wait_ge(o_rstd, 1)
        dve.wait_ge(x_again, 48)
        for t in range(3):
            n = P if t < 2 else S
            nc.vector.scalar_tensor_tensor(otok[0:n, t, :], otok[0:n, t, :], rstd[0:n, t:t + 1], gpost[0:n, :],
                                           ALU.mult, ALU.mult).then_inc(y_step, 1)
            dve.wait_ge(y_step, t + 1)
            nc.vector.tensor_tensor(otok[0:n, t, :], otok[0:n, t, :], xres[0:n, t, :],
                                    ALU.add).then_inc(y_set, 1)

    @block.gpsimd
    def _(pool):
        step = Steps(pool, pool_step)
        step(nc.gpsimd.memset(ident[:], 0.0))
        nc.gpsimd.affine_select(out=ident[:], in_=ident[:], compare_op=ALU.not_equal, fill=1.0, base=0,
                                pattern=[[-1, P]], channel_multiplier=1).then_inc(consts, 1)
        nc.gpsimd.memset(half[:], -0.5)
        nc.gpsimd.memset(onesrow[:], 1.0)
        nc.gpsimd.memset(keep_w[:], 0.0)
        nc.gpsimd.memset(mask8[:], 1.0)
        nc.gpsimd.memset(eye8[:], 0.0)
        nc.gpsimd.memset(rep32[:], 0.0)
        nc.gpsimd.memset(gq[:], 0.0)
        nc.gpsimd.memset(wgh[:].bitcast(F32), 0.0)
        nc.gpsimd.memset(wgl[:].bitcast(F32), 0.0)
        nc.gpsimd.memset(r01[:], 1.0)
        nc.gpsimd.memset(rneg[:], 0.0)
        nc.gpsimd.memset(gqs[:], 0.0)
        step(nc.gpsimd.memset(ones8[:], 1.0))

        def select(out, pattern, base, cm, fill, op=ALU.is_ge):
            step(nc.gpsimd.affine_select(out=out, in_=out, compare_op=op, fill=fill, base=base,
                                         pattern=pattern, channel_multiplier=cm))

        select(keep_w[:, 0:P], [[1, P]], 0, -1, MASKED)
        select(keep_w[:, P:], [[1, S]], 0, -1, MASKED)
        select(keep_w[:, P:].rearrange("p (b t) -> p b t", t=TS), [[-TS, NB], [0, TS]], 0, 1, MASKED)
        for g4 in range(0, P, S):
            select(mask8[g4:g4 + S], [[-TS, NB]], 0, 1, 0.0)
            select(mask8[g4:g4 + S], [[TS, NB]], TS - 1, -1, 0.0)
        select(rep32[:].rearrange("p (g s) -> p g s", s=S), [[0, P // S], [-1, S]], 0, 1, 1.0, ALU.not_equal)
        select(eye8[:], [[-1, HEADS]], 0, 1, 1.0, ALU.not_equal)
        for t, v in ((r01, 0.0), (rneg, NEVER)):
            nc.gpsimd.memset(t[:, 0:1], v)
            nc.gpsimd.memset(t[:, TP:T].rearrange("p (b t) -> p b t", t=TS)[:, :, 0:1], v)
        pool.wait_ge(x_var, 1)
        nc.gpsimd.tensor_tensor(rstd[:], stat[:], half[:], ALU.pow).then_inc(x_rstd, 1)
        pool.dma_start(wg[:], w_in.rearrange("(k p) n -> p k n", p=P)[:, :, COL_IG:COL_IG + 16]).then_inc(gin, 16)
        pool.dma_start(bg[:, 0:1], b_ig.unsqueeze(1)).then_inc(gb_in, 16)
        pool.dma_start(bg[:, 1:2], b_fg.unsqueeze(1)).then_inc(gb_in, 16)
        with nc.allow_non_contiguous_dma(reason="64 values"):
            pool.dma_start(m0[:], state_m.rearrange("b h -> h b")).then_inc(gb_in, 16)
        pool.dma_start(nrow[:], state_n.rearrange("b h d -> (b h) d")).then_inc(gb_in, 16)
        pool.wait_ge(x_t, KT)
        nc.gpsimd.memset(tri01[:], 1.0)
        step(nc.gpsimd.memset(blk01[:], 1.0))
        select(tri01[:], [[1, P]], 0, -1, 0.0)
        select(blk01[:], [[1, S]], 0, -1, 0.0)
        nc.gpsimd.affine_select(out=blk01[:].rearrange("p (b t) -> p b t", t=TS),
                                in_=blk01[:].rearrange("p (b t) -> p b t", t=TS), compare_op=ALU.is_ge,
                                fill=0.0, base=0, pattern=[[-TS, NB], [0, TS]],
                                channel_multiplier=1).then_inc(consts, 1)
        pool.dma_start(wsn[:], w_s.rearrange("g t s -> t g s")).then_inc(w_sp_in, 16)
        pool.dma_start(brow[:], b_s.unsqueeze(0)).then_inc(w_sp_in, 16)
        pool.dma_start(lng[:], ln_g.partition_broadcast(P)).then_inc(ln_in, 16)
        pool.dma_start(lnb[:], ln_b.partition_broadcast(P)).then_inc(ln_in, 16)
        pool.wait_ge(v_var, 6)
        nc.gpsimd.tensor_tensor(rstd[:], stat[:], half[:], ALU.pow).then_inc(v_rstd, 1)
        pool.wait_ge(g_rows, 1)
        with nc.allow_non_contiguous_dma(reason="72 values"):
            pool.dma_start(m_p.rearrange("o h -> h o"), gmn[:, 0:1]).then_inc(m_out, 16)
            pool.dma_start(m_s.rearrange("b h -> h b"), gmn[:, 1:]).then_inc(m_out, 16)
        with pool.Fori(0, GROUPS) as i:
            pool.wait_ge(vn_ready, i + 1)
            pool.nop(nofuse=True)
            pool.dma_start(vrows_p[0, :, ds(DH * i, DH)], vn[:, 1, :]).then_inc(vr_out, 16)
            pool.dma_start(vrows_s.rearrange("b t d -> (b t) d")[:, ds(DH * i, DH)], vn[0:S, 2, :]
                           ).then_inc(vr_out, 16)

        def load_c(h, half_):
            pool.dma_start(Cin[:, 4 * half_:4 * half_ + 4].rearrange("p b v k -> p b (v k)"),
                           Cs_in[:, 4 * half_:4 * half_ + 4, ds(h, 1)].rearrange("p b o n -> p (b o) n")).then_inc(c_in[half_], 16)

        def load_hist(h):
            pool.dma_start(hst[:], conv_in_v[:, :, ds(DH * h, DH)]).then_inc(hst_in, 16)

        def load_n(h):
            pool.dma_start(nin[:], state_n[:, ds(h, 1), :].rearrange("b o k -> (b o) k")).then_inc(n_in, 16)

        pool.wait_ge(yg_lo, GROUPS)
        pool.wait_ge(sp_used, GROUPS)
        pool.wait_ge(vr_out, 32 * GROUPS)
        load_c(0, 0)
        load_c(0, 1)
        load_hist(0)
        load_n(0)

        def h_body(h, more=True):
            pool.wait_ge(cst_ev, h + 1)
            pool.nop(nofuse=True)
            for rows, out in ((slice(0, 3), conv_p_v), (slice(3, 27), conv_s_v)):
                pool.dma_start(out[:, :, ds(DH * h, DH)], cst[rows].rearrange("r (s a) b -> r s (a b)", s=2)
                               ).then_inc(cst_out, 16)
            if more:
                load_hist(h + 1)
            pool.wait_ge(var_set, h + 1)
            nc.gpsimd.tensor_tensor(rstd[:], stat[:], half[:], ALU.pow).then_inc(rs_set, 1)
            pool.wait_ge(nn_ev, h + 1)
            pool.nop(nofuse=True)
            pool.dma_start(n_s[:, ds(h, 1), :].rearrange("b o k -> (b o) k"), nout[:, 0, :]).then_inc(nn_out, 16)
            pool.dma_start(n_p[0, ds(h, 1), :], nout[0:1, 1, :]).then_inc(nn_out, 16)
            pool.wait_ge(cp_ev, h + 1)
            pool.nop(nofuse=True)
            pool.dma_start(Cp_out[:, ds(h, 1)].rearrange("p o n -> p (o n)"),
                           cpo[:].rearrange("p v k -> p (v k)")).then_inc(cp_out, 16)
            if more:
                load_n(h + 1)
            for half_ in range(2):
                pool.wait_ge(cs_ev, 8 * h + 4 * half_ + 4)
                pool.nop(nofuse=True)
                pool.dma_start(Cs_out[:, 4 * half_:4 * half_ + 4, ds(h, 1)].rearrange("p b o n -> p (b o) n"),
                               Cin[:, 4 * half_:4 * half_ + 4].rearrange("p b v k -> p b (v k)")).then_inc(cs_out[half_], 16)
            if more:
                pool.wait_ge(cst_out, 32 * h + 32)
                pool.wait_ge(nn_out, 32 * h + 32)
                pool.wait_ge(cp_out, 16 * h + 16)
                for half_ in range(2):
                    pool.wait_ge(cs_out[half_], 16 * h + 16)
                    pool.nop(nofuse=True)
                    load_c(h + 1, half_)

        with pool.Fori(0, HEADS - 1) as h:
            h_body(h)
        h_body(HEADS - 1, more=False)
        pool.wait_ge(o_var, 6)
        nc.gpsimd.tensor_tensor(rstd[:], stat[:], half[:], ALU.pow).then_inc(o_rstd, 1)
        for s, n in ((m_out, 2), (vr_out, 16), (cst_out, 16), (nn_out, 16), (cp_out, 8), (cs_out[0], 8),
                     (cs_out[1], 8)):
            pool.wait_ge(s, 16 * n)

    block.__exit__(None, None, None)


_INS = ["x_prompt", "x_sample", "state_mlstm_C", "state_mlstm_n", "state_mlstm_m", "state_conv_qk", "g_pre", "w_in",
        "b_ig", "b_fg", "w_conv", "b_conv", "g_head", "ln_g", "ln_b", "w_s", "b_s", "w_pa", "w_pb", "w_out", "g_post"]
_OUTS = [(1, TP, D), (NB, TS, D), (1, HEADS, DH, DH), (1, HEADS, DH), (1, HEADS), (1, HIST, 2 * D), (1, P, D),
         (NB, HEADS, DH, DH), (NB, HEADS, DH), (NB, HEADS), (NB, HIST, 2 * D), (NB, TS, D)]


def kernel(**inputs):
    import numpy as np
    import concourse.bacc as bacc
    from concourse.bass_utils import run_bass_kernel_spmd

    nc = bacc.Bacc("TRN2", target_bir_lowering=False, num_devices=1)
    arrays, args = {}, []
    for name in _INS:
        arr = np.ascontiguousarray(inputs[name])
        arrays[f"in_{name}_dram"] = arr
        args.append(nc.dram_tensor(f"in_{name}_dram", arr.shape, mybir.dt.from_np(arr.dtype),
                                   kind="ExternalInput").ap())
    for n, shape in enumerate(_OUTS):
        args.append(nc.dram_tensor(f"out_{n}_dram", shape, F32, kind="ExternalOutput").ap())
    build(nc, *args)
    r = run_bass_kernel_spmd(nc, [arrays], core_ids=[0])
    return tuple(r.results[0][f"out_{n}_dram"] for n in range(len(_OUTS)))
```

```python
import concourse.bass as bass
from concourse import mybir

F32 = mybir.dt.float32
F32R = mybir.dt.float32r
ALU = mybir.AluOpType
ACT = mybir.ActivationFunctionType
ds = bass.ds

P = 128
D = 2048
KT = D // P
HEADS, DH = 8, 256
GROUPS = 8
TP, NB, TS = 256, 8, 4
S = NB * TS
T = TP + S
PW = 256
CK = 4
CHUNKS = KT // CK
CONV = 4
HIST = CONV - 1
XPS = HIST + TP
XPW = XPS + NB * (HIST + TS)
CW = XPW - HIST
HALVES = (slice(0, D // 2), slice(D // 2, D))
Y_PARTS = ([(P, 0, slice(c, c + D // 4)) for c in (0, D // 4)] + [(P, 0, slice(D // 2, D))]
           + [(P, 1, slice(c, c + D // 2)) for c in (0, D // 2)] + [(S, 2, slice(0, D))])
LO = 32
NEW_BANK = (2, 3, 5)
EPS = 1e-6
MASKED = -30000.0
NEVER = -3.0e38

COL_Q, COL_K, COL_V, COL_O, COL_ZA = (D * i for i in range(5))
COL_IG = 5 * D
COL_U = COL_IG + 2 * HEADS
COL_VB, COL_ZB, COL_GA, COL_GB = (COL_U + D * i for i in range(1, 5))

V0, G0, MB0, H0, MA0, O0 = 0, 8, 24, 40, 80, 96
V_USE, G_USE, MB_USE, H_USE, MA_USE, O_USE = (0, 0), (4, 4), (12, 12), (20, 20), (44, 36), (52, 44)
PAIRS = 104


class Steps:

    def __init__(self, eng, sem, before=0):
        self.eng, self.sem, self.before, self.n = eng, sem, before, 0

    def __call__(self, ins):
        self.n += 1
        ins.then_inc(self.sem, 1)
        self.eng.wait_ge(self.sem, self.before + self.n)


def build(nc, x_prompt, x_sample, state_C, state_n, state_m, state_conv, g_pre, w_in, b_ig, b_fg,
          w_conv, b_conv, g_head, ln_g, ln_b, w_s, b_s, w_pa, w_pb, w_out, g_post,
          y_prompt, y_sample, C_p, n_p, m_p, conv_p, vrows_p, C_s, n_s, m_s, conv_s, vrows_s):

    base = (nc.sbuf_base + 63) // 64 * 64
    limit = nc.sbuf_usable_end

    class Area:
        def __init__(self, start):
            self.at = start

        def __call__(self, name, shape, dt=F32):
            n = 4
            for s in shape[1:]:
                n *= s
            t = nc.alloc_sbuf_tensor_at(name, shape, dt, offset=self.at)
            self.at += (n + 31) // 32 * 32
            assert self.at <= limit, (name, self.at, limit)
            return t

    fixed = Area(base)
    xh = fixed("xh", [P, KT, T], F32R)
    xl = fixed("xl", [P, KT, T], F32R)
    raw = fixed("raw", [P, CHUNKS, CK, PW])
    whi = fixed("whi", [P, CHUNKS, CK, PW], F32R)
    wlo = fixed("wlo", [P, CHUNKS, CK, PW], F32R)
    ident = fixed("ident", [P, P])
    keep_w = fixed("keep_w", [P, P + S])
    mask8 = fixed("mask8", [P, NB])
    eye8 = fixed("eye8", [LO + HEADS, HEADS])
    par0 = fixed("par0", [P, P])
    par1 = fixed("par1", [P, 64])
    ghh = fixed("ghh", [P, 16])
    rstd = fixed("rstd", [P, 3])
    stat = fixed("stat", [P, 3])
    gq = fixed("gq", [P, 3, 96])
    nb = fixed("nb", [LO + HEADS, T + S], F32R)
    wsr = fixed("wsr", [LO + HEADS, T], F32R)
    dec_bc = fixed("dec_bc", [P, HEADS * NB])
    nacc = fixed("nacc", [P, 2, NB + 1, HEADS])
    nTh = fixed("nTh", [P, 2, NB * HEADS], F32R)
    nTl = fixed("nTl", [P, 2, NB * HEADS], F32R)
    half = fixed("half", [P, 3])
    yarea = fixed.at
    y_ = Area(yarea)
    yh = y_("yh", [P, KT, T], F32R)
    yl = y_("yl", [P, KT, T], F32R)
    phase = y_.at

    a = Area(phase)
    xt = a("xt", [P, 3, D])
    hb0 = a("hb0", [P, 3, D])
    prow = a("prow", [P, 2, P])
    a = Area(phase)
    vtok = a("vtok", [P, 3, D])
    lng = a("lng", [P, D])
    lnb = a("lnb", [P, D])
    wsn = a("wsn", [P, GROUPS, P])
    bsb = a("bsb", [P, GROUPS, P])
    a = Area(max(a.at, phase + 2 * 3 * D * 4 + 1024 + 64))
    wsT = a("wsT", [P, GROUPS, P])
    b = Area(a.at)
    vf = b("vf", [P, 2, 2, T])
    vn = b("vn", [P, 3, DH])
    uf = b("uf", [P, 2, T])
    zs_g = b("zs_g", [P, 2, T])
    tt_g = b("tt_g", [P, 2, T])
    yf_g = b("yf_g", [P, 2, T])
    rep4 = b("rep4", [TS, S])
    wd = b("wd", [S, GROUPS, S])
    tri01 = b("tri01", [P, P])
    blk01 = b("blk01", [S, S])
    vstat = b("vstat", [P, 3, 8, 6])
    mv = b("mv", [P, 3, 2])
    nmu = b("nmu", [P, 3])
    ypost_end = b.at
    g = Area(yarea)
    wg = g("wg", [P, KT, 16])
    wg2 = g("wg2", [P, KT, 104], F32R)
    bg = g("bg", [HEADS, 2])
    m0 = g("m0", [HEADS, NB])
    nrow = g("nrow", [NB * HEADS, DH])
    r01 = g("r01", [HEADS, T])
    rneg = g("rneg", [HEADS, T])
    gi = g("gi", [HEADS, T])
    gf = g("gf", [HEADS, T])
    gab = g("gab", [HEADS, T])
    gln = g("gln", [HEADS, T])
    glf = g("glf", [HEADS, T])
    gbc = g("gbc", [HEADS, T])
    ga_ = g("ga_", [HEADS, T])
    gd1 = g("gd1", [HEADS, T])
    gM = g("gM", [HEADS, T])
    gx = g("gx", [HEADS, 2 * T + S + NB])
    gy = g("gy", [HEADS, 2 * T + S + NB])
    gqs = g("gqs", [96, T])
    gqs4 = g("gqs4", [96, P])
    gdx = g("gdx", [HEADS, HEADS, NB])
    gmn = g("gmn", [HEADS, 1 + NB])
    ones8 = g("ones8", [HEADS, P])
    assert g.at <= phase
    a = Area(phase)
    part = a("part", [P, KT, T])
    after_part = a.at
    a = Area(after_part)
    Cin = a("Cin", [P, NB, 2, DH])
    CTh = a("CTh", [P, 2, DH + 2], F32R)
    CTl = a("CTl", [P, 2, DH + 2], F32R)
    ktok = a("ktok", [P, 3, DH])
    vtok_h = a("vtok_h", [P, 3, DH + 1])
    kst = a("kst", [P, DH], F32R)
    vst = a("vst", [P, DH], F32R)
    W = a("W", [P, 416])
    scb = a("scb", [P, 2, S])
    qk = a("qk", [P, 4, T])
    vm = nc.alloc_sbuf_tensor_at("vm", [P, 4, XPW], F32R, offset=a.at)[:, :, 4:4 + DH]
    xp = a("xp", [P, 4, XPW])
    kv4 = a("kv4", [P, 2, 2, P])
    hb = a("hb", [P, 3, DH])
    acc = hb[:].rearrange("p t d -> p (t d)")[:, 0:2 * XPW].rearrange("p (j c) -> p j c", j=2)
    vz = a("vz", [P, 2, T])
    og = a("og", [P, 2, T])
    tg = og
    wsb = og[:, 0, :]
    yf = og
    qm = a("qm", [P, 2, S + NB * (2 * S + TS)], F32R)
    cpo = a("cpo", [P, 2, DH])
    cn = a("cn", [P, 4, 27])
    cst = a("cst", [27, 4, P])
    hst = a("hst", [24, 2, DH])
    bcrow = a("bcrow", [LO + HEADS, T + S], F32R)
    ones8h = a("ones8h", [LO + HEADS, P], F32R)
    r3 = a("r3", [P, 3])
    q3 = a("q3", [P, 3])
    f3 = a("f3", [P, 3])
    a = Area(after_part)
    tm = a("tm", [P, 2, T])
    sm = a("sm", [P, 2, T])
    mh = a("mh", [P, KT, T], F32R)
    ml = a("ml", [P, KT, T], F32R)
    a = Area(phase)
    vf_o = a("vf_o", [P, 2, 2, T])
    assert a.at <= after_part
    a = Area(yarea)
    otok = a("otok", [P, 3, D])
    gpost = a("gpost", [P, D])
    assert a.at <= phase
    xres = Area(base)("xres", [P, 3, D])
    a = Area(phase + 2 * 2 * T * 4)
    osq = a("osq", [P, 3, 8])
    squared = a("squared", [P, 3, PW])
    nout = a("nout", [(NB + 1) * HEADS, DH])

    ps = nc.alloc_psum_tensor("ps", [P, 8, 512], F32)

    def sem(name):
        return nc.alloc_semaphore(name)

    raw_landed = [sem(f"raw_landed{c}") for c in range(CHUNKS)]
    hi_ready, lo_ready, chunk_done = sem("hi_ready"), sem("lo_ready"), sem("chunk_done")
    slot_free = [sem("slot0_free"), sem("slot1_free")]
    x_in, par_in, gin, w_sp_in, ln_in = ([sem(f"x_in{t}") for t in range(3)], sem("par_in"), sem("gin"),
                                         sem("w_sp_in"), sem("ln_in"))
    x_norm_a = sem("x_norm_a")
    ws_row, wsb_mm, wsb_set, n_step = sem("ws_row"), sem("wsb_mm"), sem("wsb_set"), sem("n_step")
    n_turn, n_rows, tt_set = sem("n_turn"), sem("n_rows"), sem("tt_set")
    gw_zero, g_in, table_in = sem("gw_zero"), sem("g_in"), sem("table_in")
    consts, const_v, par_t, par_set = sem("consts"), sem("const_v"), sem("par_t"), sem("par_set")
    x_sq, x_var, x_rstd, x_norm, x_t, x_hi, x_lo = (sem(n) for n in (
        "x_sq", "x_var", "x_rstd", "x_norm", "x_t", "x_hi", "x_lo"))
    vf_set, tok_t, tok_ev = sem("vf_set"), sem("tok_t"), sem("tok_ev")
    of_set, otok_t, otok_ev = sem("of_set"), sem("otok_t"), sem("otok_ev")
    gw_hi, gw_lo, g_mm, g_dve, g_act_in, g_act = (sem(n) for n in (
        "gw_hi", "gw_lo", "g_mm", "g_dve", "g_act_in", "g_act"))
    g_rows, g_t, g_set, ws_t, ws_set, v_var, v_rstd, m_out = (sem(n) for n in (
        "g_rows", "g_t", "g_set", "ws_t", "ws_set", "v_var", "v_rstd", "m_out"))
    gb_in, pool_step = sem("gb_in"), sem("pool_step")
    vn_step, vn_ready, sp_mm, sp_used, yg_ready, yg_hi, vr_out, yg_lo = (sem(n) for n in (
        "vn_step", "vn_ready", "sp_mm", "sp_used", "yg_ready", "yg_hi", "vr_out", "yg_lo"))
    ma_sum, ma_hi, ma_lo = sem("ma_sum"), sem("ma_hi"), sem("ma_lo")
    h_const = sem("h_const")
    hst_in, c_in = sem("hst_in"), [sem("c_in0"), sem("c_in1")]
    hist_t, hist_set, bc_row, bc_mm, w_arg, w_exp = (sem(n) for n in (
        "hist_t", "hist_set", "bc_row", "bc_mm", "w_arg", "w_exp"))
    q_ev, k_ev, v_ev, conv_step, silu_q, silu_k, qm_set = (sem(n) for n in (
        "q_ev", "k_ev", "v_ev", "conv_step", "silu_q", "silu_k", "qm_set"))
    ct_t, ct_ev, s_mm, p_set, cn_set, cn_t, cst_ev = (sem(n) for n in (
        "ct_t", "ct_ev", "s_mm", "p_set", "cn_set", "cn_t", "cst_ev"))
    kt_t, kt_ev, kvs_t, kvs_ev, vt_t, vt_ev, num_mm, den_step, r_set, sq_set, var_set, rs_set, f_set = (
        sem(n) for n in ("kt_t", "kt_ev", "kvs_t", "kvs_ev", "vt_t", "vt_ev", "num_mm", "den_step", "r_set",
                         "sq_set", "var_set", "rs_set", "f_set"))
    h_set, ht_t, z_set, gate_set, yf_set, ya_hi, cp_mm, cp_ev, nn_ev, vm_set, cs_mm, cs_ev = (
        sem(n) for n in ("h_set", "ht_t", "z_set", "gate_set", "yf_set", "ya_hi", "cp_mm", "cp_ev",
                         "nn_ev", "vm_set", "cs_mm", "cs_ev"))
    q_step, ct_lo, lo_rows = sem("q_step"), sem("ct_lo"), sem("lo_rows")
    inter_mm = sem("inter_mm")
    ya_lo, st_lo, kv4_set = sem("ya_lo"), sem("st_lo"), sem("kv4_set")
    cst_out, cp_out, nn_out, cs_out = sem("cst_out"), sem("cp_out"), sem("nn_out"), [sem("cs_out0"), sem("cs_out1")]
    x_again, g_post_in, o_sq, osq_set, o_var, o_rstd, y_set, y_out = (sem(n) for n in (
        "x_again", "g_post_in", "o_sq", "osq_set", "o_var", "o_rstd", "y_set", "y_out"))

    def chunked(w):
        return w.rearrange("(c k p) n -> c p k n", k=CK, p=P)

    w_in_v, w_pa_v, w_pb_v, w_out_v = (chunked(w) for w in (w_in, w_pa, w_pb, w_out))
    xp_v = x_prompt.rearrange("o (n p) d -> p (o n) d", p=P)
    xs_v = x_sample.rearrange("b t d -> (b t) d")
    Cs_in = state_C.rearrange("b h (p v) k -> p b h (v k)", p=P)
    Cs_out = C_s.rearrange("b h (p v) k -> p b h (v k)", p=P)
    Cp_out = C_p.rearrange("o h (p v) k -> p (o h) (v k)", p=P)
    conv_in_v = state_conv.rearrange("b r (s n) -> (b r) s n", s=2)
    conv_p_v = conv_p.rearrange("o r (s n) -> (o r) s n", s=2)
    conv_s_v = conv_s.rearrange("b r (s n) -> (b r) s n", s=2)

    block = nc.Block()
    block.__enter__()

    def x_bank(k):
        return k if k < 8 else 4 + k % 4

    def turned(b):
        return ps[:, 6 + b % 2, :].rearrange("p (k v q) -> p k v q", k=2, v=2)

    def key_major(t):
        return t[:, :, 0:DH].rearrange("p k (q v) -> p k v q", v=2)

    @block.sync
    def _(sp):
        for t in range(2):
            sp.dma_start(xt[:, t, :], xp_v[:, t, :]).then_inc(x_in[t], 16)
        sp.dma_start(xt[0:S, 2, :], xs_v).then_inc(x_in[2], 16)
        sp.dma_start(prow[:, 0, :], w_conv.rearrange("j (n p) -> (j n) p", p=P)).then_inc(par_in, 16)
        sp.dma_start(prow[0:32, 1, :], b_conv.rearrange("(n p) -> n p", p=P)).then_inc(par_in, 16)
        sp.dma_start(prow[32:48, 1, :], g_pre.rearrange("(n p) -> n p", p=P)).then_inc(par_in, 16)
        sp.dma_start(prow[48:64, 1, :], g_head.rearrange("h (n p) -> (h n) p", p=P)).then_inc(par_in, 16)

        def load_pair(pair, w, col, first=False):
            for c in range(CHUNKS):
                if not first:
                    sp.wait_ge(lo_ready, 4 * pair - 3 + c)
                    sp.nop(nofuse=True)
                sp.dma_start(raw[:, c], w[c, :, :, ds(col, PW)]).then_inc(raw_landed[c], 16)

        load_pair(V0, w_in_v, COL_VB, first=True)
        with sp.Fori(1, 8) as i:
            load_pair(V0 + i, w_in_v, COL_VB + PW * i)
        with sp.Fori(0, GROUPS) as i:
            load_pair(G0 + 2 * i, w_in_v, COL_U + PW * i)
            load_pair(G0 + 1 + 2 * i, w_in_v, COL_ZB + PW * i)
        with sp.Fori(0, 8) as i:
            load_pair(MB0 + 2 * i, w_in_v, COL_GB + PW * i)
            load_pair(MB0 + 1 + 2 * i, w_pb_v, PW * i)
        with sp.Fori(0, HEADS) as h:
            for j, col in enumerate((COL_Q, COL_K, COL_V, COL_O, COL_ZA)):
                load_pair(H0 + j + 5 * h, w_in_v, col + PW * h)
        with sp.Fori(0, 8) as i:
            load_pair(MA0 + 2 * i, w_in_v, COL_GA + PW * i)
            load_pair(MA0 + 1 + 2 * i, w_pa_v, PW * i)
        for i in range(2):
            load_pair(O0 + i, w_out_v, PW * i)
        sp.wait_ge(chunk_done, 4 * O0)
        sp.dma_start(gpost[:], g_post.partition_broadcast(P)).then_inc(g_post_in, 16)
        with sp.Fori(2, 8) as i:
            load_pair(O0 + i, w_out_v, PW * i)
        sp.dma_start(xres[:, 0:2, :], xp_v).then_inc(x_again, 16)
        sp.dma_start(xres[0:S, 2, :], xs_v).then_inc(x_again, 16)
        y_rows = (y_prompt[0, 0:P, :], y_prompt[0, P:TP, :], y_sample.rearrange("b t d -> (b t) d"))
        for k, (n, t, cols) in enumerate(Y_PARTS):
            sp.wait_ge(y_set, k + 1)
            sp.dma_start(y_rows[t][:, cols], otok[0:n, t, cols]).then_inc(y_out, 16)
        sp.wait_ge(y_out, 16 * len(Y_PARTS))

    @block.tensor
    def _(pe):
        def chunk(pair, c, slot, free, mh_, ml_):
            pe.wait_ge(lo_ready, 4 * pair + (c + 1))
            if c == 0 and free is not None:
                pe.wait_ge(slot_free[slot], free)
            for kk in range(CK):
                k = CK * c + kk
                for j in range(2):
                    out = ps[:, 2 * slot + j, 0:T]
                    cols = slice(P * j, P * j + P)
                    nc.tensor.matmul(out, whi[:, c, kk, cols], mh_[:, k, :], start=(k == 0), stop=False)
                    nc.tensor.matmul(out, whi[:, c, kk, cols], ml_[:, k, :], start=False, stop=False)
                    last = nc.tensor.matmul(out, wlo[:, c, kk, cols], mh_[:, k, :], start=False,
                                            stop=(k == KT - 1))
            last.then_inc(chunk_done, 1)

        def turn(out_bank, src, j):
            for t in range(2):
                pe.transpose(ps[:, out_bank, PW * t + P * j:PW * t + P * j + P],
                             src[:, j, P * t:P * t + P], ident[:])
            return pe.transpose(ps[0:S, out_bank + 1, P * j:P * j + P], src[:, j, TP:T], ident[:])

        pe.wait_ge(par_in, 64)
        pe.wait_ge(consts, 1)
        pe.transpose(ps[:, 6, 0:P], prow[:, 0, :], ident[:])
        pe.transpose(ps[:, 6, P:P + 64], prow[0:64, 1, :], ident[0:64, 0:64]).then_inc(par_t, 1)
        def turn_x(k0, k1):
            for k in range(k0, k1):
                if k % 8 == 0:
                    pe.wait_ge(x_norm_a, k // 8 + 1)
                    pe.wait_ge(x_norm, 2 * (k // 8) + 2)
                if k == 6:
                    pe.wait_ge(par_set, 1)
                if k >= 8:
                    pe.wait_ge(x_lo, k - 3)
                for t in range(2):
                    pe.transpose(ps[:, x_bank(k), P * t:P * t + P], hb0[:, t, P * k:P * k + P], ident[:])
                pe.transpose(ps[:, x_bank(k), TP:T], hb0[0:S, 2, P * k:P * k + P],
                             ident[0:S, 0:S]).then_inc(x_t, 1)

        def gate_sums():
            pe.wait_ge(gw_lo, 2)
            for k in range(KT):
                nc.tensor.matmul(ps[0:104, 4, 0:T], wg2[:, k, :], xh[:, k, :], start=(k == 0), stop=False)
                last = nc.tensor.matmul(ps[0:104, 4, 0:T], wg2[:, k, :], xl[:, k, :], start=False,
                                        stop=(k == KT - 1))
            last.then_inc(g_mm, 1)

        def turn_w_s():
            pe.wait_ge(w_sp_in, 32)
            for q in range(GROUPS):
                last = pe.transpose(ps[:, 6 + q // 4, P * (q % 4):P * (q % 4) + P], wsn[:, q, :], ident[:])
            last.then_inc(ws_t, 1)

        def w_s_corners():
            pe.wait_ge(ws_set, 2)
            nc.tensor.matmul(ps[0:S, 6, 0:S], rep4[:],
                             wsT[0:TS, :, 0:TS], start=True, stop=True).then_inc(ws_t, 1)

        def gates():
            pe.wait_ge(g_rows, 1)
            for t in range(2):
                pe.transpose(ps[:, 5, 256 + 96 * t:352 + 96 * t], gqs[:, P * t:P * t + P], ident[0:96, 0:96])
            nc.tensor.matmul(ps[:, 5, 448:512], ones8[:], gdx[:].rearrange("p a b -> p (a b)"),
                             start=True, stop=True)
            pe.transpose(ps[:, 7, 256:352], gqs4[:], ident[0:96, 0:96])
            for j in range(2):
                last = pe.transpose(ps[:, 7, 384 + 64 * j:448 + 64 * j], nrow[:, P * j:P * j + P],
                                    ident[0:64, 0:64])
            last.then_inc(g_t, 1)

        def turn_v(s, pair, reused=True):
            pe.wait_ge(vf_set, pair + 1)
            if reused:
                pe.wait_ge(tok_ev, pair - 1)
            turn(4 + 2 * s, vf[:, s], 0)
            turn(4 + 2 * s, vf[:, s], 1).then_inc(tok_t, 1)

        def v_body(i, first=False, second=False):
            for s in range(2):
                for c in range(CHUNKS):
                    if first and s == 0:
                        pe.wait_ge(x_lo, CK * (c + 1))
                    chunk(V0 + s + 2 * i, c, s, None if first else i, xh, xl)
                    if first and s == 0 and c < 2:
                        turn_x(8 + CK * c, 8 + CK * (c + 1))
                    if first and (s, c) == (0, 3):
                        gate_sums()
                    if first and (s, c) == (1, 0):
                        turn_w_s()
                    if c == 1 and not (first and s == 0):
                        if first:
                            pe.wait_ge(g_in, 1)
                        if second and s == 0:
                            pe.wait_ge(ws_set, 3)
                        if not (first or second):
                            pe.wait_ge(g_set, 1)
                        turn_v(1 - s, 2 * i + s - 1, reused=not (first or second and s == 0))
                    if first and (s, c) == (1, 2):
                        w_s_corners()
                    if second and (s, c) == (1, 3):
                        pe.wait_ge(tok_ev, 3)
                        gates()

        turn_x(0, 8)
        v_body(0, first=True)
        v_body(1, second=True)
        with pe.Fori(2, 4) as i:
            v_body(i)

        def g_body(i, first=False):
            for c in range(CHUNKS):
                chunk(G0 + 2 * i, c, 0, G_USE[0] + i, xh, xl)
                if first and c == 0:
                    turn_v(1, 7)
                if c == (3 if first else 2):
                    pe.wait_ge(vn_ready, i + 1)
                    if first:
                        pe.wait_ge(tok_ev, 8)
                    else:
                        pe.wait_ge(sp_used, i)
                    for j in range(2):
                        cols = slice(P * j, P * j + P)
                        for t in range(2):
                            nc.tensor.matmul(ps[:, 4 + j, P * t:P * t + P], vn[:, t, cols],
                                             wsT[:, ds(i, 1), :].squeeze(1), start=True, stop=True)
                        last = nc.tensor.matmul(ps[:, 4 + j, TP:T], vn[0:S, 2, cols], wd[:, ds(i, 1), :].squeeze(1),
                                                start=True, stop=True)
                    last.then_inc(sp_mm, 1)
            for c in range(CHUNKS):
                chunk(G0 + 1 + 2 * i, c, 1, G_USE[1] + i, xh, xl)

        g_body(0, first=True)
        with pe.Fori(1, GROUPS) as i:
            g_body(i)

        with pe.Fori(0, 8) as i:
            for c in range(CHUNKS):
                chunk(MB0 + 2 * i, c, 0, MB_USE[0] + i, xh, xl)
            pe.wait_ge(yg_lo, GROUPS)
            for c in range(CHUNKS):
                chunk(MB0 + 1 + 2 * i, c, 1, MB_USE[1] + i, yh, yl)

        X4, X5, X6, X7 = 4, 5, 6, 7

        def c_turn(h, b):
            if b % 4 == 0:
                pe.wait_ge(c_in[b // 4], 16 * h + 16)
            if b >= 2:
                pe.wait_ge(ct_lo, 8 * h + b - 1)
            for kh in range(2):
                for vh in range(2):
                    last = pe.transpose(ps[:, X6 + b % 2, DH * kh + P * vh:DH * kh + P * vh + P],
                                        Cin[:, b, vh, P * kh:P * kh + P], ident[:])
            last.then_inc(ct_t, 1)

        def inter(h, b):
            pe.wait_ge(ct_lo, 8 * h + b + 1)
            if b == 0:
                pe.wait_ge(qm_set, h + 1)
            for kh in range(2):
                for part_ in (CTh, CTl):
                    last = nc.tensor.matmul(ps[0:2 * S, X4, 0:DH + 2], qm[:, kh, 2 * S * b:2 * S * b + 2 * S],
                                            part_[:, kh, :], start=(b == 0 and kh == 0 and part_ is CTh),
                                            stop=(b == NB - 1 and kh == 1 and part_ is CTl),
                                            skip_group_check=True)
            last.then_inc(inter_mm, 1)

        def new_state(h, b):
            pe.wait_ge(vm_set, 8 * h + b + 1)
            if b >= 3:
                pe.wait_ge(cs_ev, 8 * h + b - 2)
            for vh in range(2):
                last = nc.tensor.matmul(ps[:, NEW_BANK[b % 3], DH * vh:DH * vh + DH],
                                        vm[:, b % 4, vh::2], kst[:], start=True, stop=True)
            last.then_inc(cs_mm, 1)

        with pe.Fori(0, HEADS) as h:
            for c in range(CHUNKS):
                chunk(H0 + 5 * h, c, 0, H_USE[0] + 3 * h, xh, xl)
                if c == 1:
                    pe.wait_ge(hst_in, 16 * h + 16)
                    pe.wait_ge(bc_row, h + 1)
                    pe.nop(nofuse=True)
                    for b in range(4):
                        last = pe.transpose(ps[:, X4, 24 * b:24 * b + 24],
                                            hst[:, b // 2, P * (b % 2):P * (b % 2) + P], ident[0:24, 0:24])
                    last.then_inc(hist_t, 1)
                if c == 2:
                    pe.wait_ge(hi_ready, 4 * (H0 + 1) + 1 + 20 * h)
                    nc.tensor.matmul(ps[:, X5, 0:T + S], ones8h[:], bcrow[:], start=True, stop=True
                                     ).then_inc(bc_mm, 1)
            for c in range(CHUNKS):
                chunk(H0 + 1 + 5 * h, c, 1, H_USE[1] + 2 * h, xh, xl)
                if c == 0:
                    pe.wait_ge(hist_set, h + 1)
                    pe.wait_ge(ws_row, h + 1)
                    nc.tensor.matmul(ps[:, X4, 0:T], ones8h[:], bcrow[:, 0:T], start=True, stop=True
                                     ).then_inc(wsb_mm, 1)
            pe.wait_ge(wsb_set, h + 1)
            for c in range(CHUNKS):
                chunk(H0 + 2 + 5 * h, c, 0, H_USE[0] + 1 + 3 * h, xh, xl)
                if c >= 1:
                    inter(h, c - 1)
                c_turn(h, c)
            for c in range(CHUNKS):
                chunk(H0 + 3 + 5 * h, c, 1, H_USE[1] + 1 + 2 * h, xh, xl)
                if c == 0:
                    pe.wait_ge(silu_k, 3 * h + 3)
                    pe.wait_ge(w_arg, h + 1)
                    for (lo, n, t0, at) in ((0, P, 0, 0), (P, P, P, TP), (TP, S, TP, 384)):
                        t1 = TP if lo < TP else T
                        for j in range(2):
                            last = nc.tensor.matmul(ps[0:n, X5, at:at + t1 - t0], qk[:, 2 + j, lo:lo + n],
                                                    qk[:, j, t0:t1], start=(j == 0), stop=(j == 1))
                    last.then_inc(s_mm, 1)
                if c == 1:
                    pe.wait_ge(cn_set, h + 1)
                    pe.wait_ge(p_set, h + 1)
                    for b in range(4):
                        last = pe.transpose(ps[0:27, X5, P * b:P * b + P], cn[:, b, :], ident[:])
                    last.then_inc(cn_t, 1)
                if c == 2:
                    pe.wait_ge(cst_ev, h + 1)
                    for j in range(2):
                        for t in range(2):
                            last = pe.transpose(ps[:, X5, DH * t + P * j:DH * t + P * j + P],
                                                qk[:, 2 + j, P * t:P * t + P], ident[:])
                    last.then_inc(kt_t, 1)
                if c == 3:
                    pe.wait_ge(kt_ev, h + 1)
                    pe.wait_ge(kv4_set, 2 * h + 2)
                    for j in range(2):
                        pe.transpose(ps[:, X5, P * j:P * j + P], kv4[:, 0, j, :], ident[:])
                        last = pe.transpose(ps[:, X5, DH + P * j:DH + P * j + P],
                                            kv4[:, 1, j, :], ident[:])
                    last.then_inc(kvs_t, 1)
                inter(h, 3 + c)
                c_turn(h, 4 + c)
            for c in range(CHUNKS):
                chunk(H0 + 4 + 5 * h, c, 0, H_USE[0] + 2 + 3 * h, xh, xl)
                if c == 0:
                    inter(h, 7)
                    pe.wait_ge(v_ev, h + 1)
                    pe.wait_ge(st_lo, h + 1)
                    for j in range(2):
                        for t in range(2):
                            last = pe.transpose(ps[:, X5, DH * t + P * j:DH * t + P * j + P],
                                                vz[:, j, P * t:P * t + P], ident[:])
                    last.then_inc(vt_t, 1)
                    pe.wait_ge(slot_free[1], H_USE[1] + 2 + 2 * h)
                    for b in range(2):
                        new_state(h, b)
                if c == 1:
                    pe.wait_ge(lo_rows, h + 1)
                    pe.wait_ge(vt_ev, h + 1)
                    nc.tensor.matmul(ps[:, X6, 0:DH + 1], W[:, 0:P], vtok_h[:, 0, :], start=True, stop=True)
                    nc.tensor.matmul(ps[:, X7, 0:DH + 1], W[:, P:TP], vtok_h[:, 0, :], start=True, stop=False)
                    nc.tensor.matmul(ps[:, X7, 0:DH + 1], W[:, TP:TP + P], vtok_h[:, 1, :], start=False,
                                     stop=True)
                    nc.tensor.matmul(ps[0:S, X4, 0:DH + 1], W[0:2 * S, 384:416], vtok_h[0:2 * S, 2, :],
                                     start=False, stop=True, skip_group_check=True).then_inc(num_mm, 1)
                    for b in range(2, 4):
                        new_state(h, b)
                if c == 2:
                    for b in range(4, 6):
                        new_state(h, b)
                if c == 3:
                    pe.wait_ge(h_set, h + 1)
                    for j in range(2):
                        for t in range(2):
                            pe.transpose(ps[:, X6 + j, P * t:P * t + P], hb[:, t, P * j:P * j + P], ident[:])
                        last = pe.transpose(ps[:, X6 + j, TP:T], hb[0:S, 2, P * j:P * j + P],
                                            ident[0:S, 0:S])
                    last.then_inc(ht_t, 1)
                    for b in range(6, NB):
                        new_state(h, b)
                    pe.wait_ge(cs_ev, 8 * h + 6)
                    for vh in range(2):
                        for t in range(2):
                            last = nc.tensor.matmul(ps[:, X5, DH * vh:DH * vh + DH], vtok_h[:, t, vh:DH:2],
                                                    ktok[:, t, :], start=(t == 0), stop=(t == 1))
                    last.then_inc(cp_mm, 1)

        with pe.Fori(0, 8) as i:
            for c in range(CHUNKS):
                chunk(MA0 + 2 * i, c, 0, MA_USE[0] + i, xh, xl)
            pe.wait_ge(cs_ev, 8 * HEADS)
            pe.wait_ge(ya_lo, HEADS)
            for c in range(CHUNKS):
                chunk(MA0 + 1 + 2 * i, c, 1, MA_USE[1] + i, yh, yl)

        def turn_o(s, pair, reused=True):
            pe.wait_ge(of_set, pair + 1)
            if reused:
                pe.wait_ge(otok_ev, pair - 1)
            turn(4 + 2 * s, vf_o[:, s], 0)
            turn(4 + 2 * s, vf_o[:, s], 1).then_inc(otok_t, 1)

        def o_body(i, first=False, second=False):
            for s in range(2):
                for c in range(CHUNKS):
                    if first and s == 0:
                        pe.wait_ge(ma_lo, 2 * c + 2)
                    chunk(O0 + s + 2 * i, c, s, O_USE[s] + i, mh, ml)
                    if c == 1 and not (first and s == 0):
                        if second and s == 0:
                            pe.wait_ge(n_rows, 1)
                        turn_o(1 - s, 2 * i + s - 1, reused=not (first or second and s == 0))
                    if first and (s, c) == (1, 2):
                        for kh in range(2):
                            last = pe.transpose(ps[0:(NB + 1) * HEADS, 6, P * kh:P * kh + P],
                                                nacc[:, kh].rearrange("p b h -> p (b h)"), ident[:])
                        last.then_inc(n_turn, 1)

        o_body(0, first=True)
        o_body(1, second=True)
        with pe.Fori(2, 4) as i:
            o_body(i)
        turn_o(1, 7)

    @block.scalar
    def _(act):
        def split_hi(pair, c, first=False):
            act.wait_ge(raw_landed[c], 16 * pair + 16)
            if not first:
                act.wait_ge(chunk_done, 4 * pair - 3 + c)
            nc.scalar.activation(whi[:, c], raw[:, c], ACT.Copy).then_inc(hi_ready, 1)

        def results(slot):
            return ps[:, 2 * slot:2 * slot + 2, 0:T]

        act.wait_ge(const_v, 1)
        nc.scalar.activation(hb0[:, 0, 0:1], stat[:, 0:1], ACT.Square).then_inc(table_in, 1)
        act.wait_ge(table_in, 1)
        for t in (0, 2):
            n = P if t < 2 else S
            act.wait_ge(x_in[t], 16)
            nc.scalar.activation(hb0[0:n, t, :], xt[0:n, t, :], ACT.Square,
                                 accum_out=stat[0:n, t:t + 1]).then_inc(x_sq, 1)
        split_hi(0, 0, first=True)
        act.wait_ge(x_rstd, 1)
        for cols in HALVES:
            nc.scalar.activation(hb0[:, 0, cols], xt[:, 0, cols], ACT.Identity,
                                 scale=rstd[:, 0:1]).then_inc(x_norm_a, 1)
        act.wait_ge(par_set, 1)
        for k in range(KT):
            act.wait_ge(x_t, k + 1)
            nc.scalar.activation(xh[:, k, :], ps[:, x_bank(k), 0:T], ACT.Identity,
                                 scale=par1[:, 32 + k:33 + k]).then_inc(x_hi, 1)
            if k % CK == CK - 1 and k < KT - 1:
                split_hi(0, k // CK + 1, first=True)
        act.wait_ge(gin, 16)
        act.wait_ge(gw_zero, 1)
        nc.scalar.activation(wg2[:, :, 0:8], wg[:, :, 0:8], ACT.Copy).then_inc(gw_hi, 1)
        nc.scalar.activation(wg2[:, :, 32:40], wg[:, :, 8:16], ACT.Copy).then_inc(gw_hi, 1)

        def v_body(i, first=False, second=False):
            for s in range(2):
                pair = V0 + s + 2 * i
                for c in range(CHUNKS):
                    split_hi(pair + 1, c)
                    if first and (s, c) == (1, 1):
                        act.wait_ge(g_act_in, 1)
                        nc.scalar.activation(gln[:], gab[:], ACT.Exp, scale=-1.0).then_inc(g_act, 1)
                        act.wait_ge(g_act, 1)
                        nc.scalar.activation(gln[:], gln[:], ACT.Ln, bias=1.0).then_inc(g_act, 1)
                    if second and (s, c) == (0, 2):
                        act.wait_ge(g_act_in, 2)
                        nc.scalar.activation(gy[:], gx[:], ACT.Exp).then_inc(g_act, 1)
                if not first:
                    act.wait_ge(tok_t, 2 * i + s - 1)
                nc.scalar.activation(vf[:, s], results(s), ACT.Copy).then_inc(vf_set, 1)
                act.wait_ge(vf_set, 2 * i + s + 1)
                act.sem_inc(slot_free[s], 1)

        v_body(0, first=True)
        v_body(1, second=True)
        with act.Fori(2, 4) as i:
            v_body(i)

        def g_body(i, first=False):
            for c in range(CHUNKS):
                split_hi(G0 + 1 + 2 * i, c)
            if not first:
                act.wait_ge(tt_set, i)
            nc.scalar.activation(uf[:], results(0), ACT.Copy).then_inc(slot_free[0], 1)
            for c in range(CHUNKS):
                split_hi(G0 + 2 + 2 * i, c)
            nc.scalar.activation(zs_g[:], results(1), ACT.Silu).then_inc(slot_free[1], 1)
            act.wait_ge(yg_ready, i + 1)
            nc.scalar.activation(yh[:, ds(2 * i, 2), :], yf_g[:], ACT.Copy).then_inc(yg_hi, 1)

        g_body(0, first=True)
        with act.Fori(1, GROUPS) as i:
            g_body(i)

        with act.Fori(0, 8) as i:
            for c in range(CHUNKS):
                split_hi(MB0 + 1 + 2 * i, c)
            act.wait_ge(slot_free[1], MB_USE[1] + i)
            nc.scalar.activation(tg[:], results(0), ACT.Tanh, scale=0.5).then_inc(slot_free[0], 1)
            for c in range(CHUNKS):
                split_hi(MB0 + 2 + 2 * i, c)

        def to_padded(j, slot, done):
            nc.scalar.activation(xp[:, j:j + 2, HIST:XPS], ps[:, 2 * slot:2 * slot + 2, 0:TP],
                                 ACT.Copy).then_inc(done, 1)
            for jj in range(2):
                last = nc.scalar.activation(
                    xp[:, j + jj, XPS:XPW].rearrange("p (b t) -> p b t", t=HIST + TS)[:, :, HIST:],
                    ps[:, 2 * slot + jj, TP:T].rearrange("p (b t) -> p b t", t=TS), ACT.Copy)
                last.then_inc(done, 1)

        def silu(j, done):
            nc.scalar.activation(qk[:, j:j + 2, 0:TP], acc[:, :, 0:TP], ACT.Silu).then_inc(done, 1)
            for jj in range(2):
                nc.scalar.activation(
                    qk[:, j + jj, TP:T].rearrange("p (b t) -> p b t", t=TS),
                    acc[:, jj, XPS:XPW].rearrange("p (b t) -> p b t", t=HIST + TS)[:, :, 0:TS],
                    ACT.Silu).then_inc(done, 1)

        def ct_copy(h, b):
            act.wait_ge(ct_t, 8 * h + b + 1)
            nc.scalar.activation(key_major(CTh), turned(b), ACT.Copy).then_inc(ct_ev, 1)

        with act.Fori(0, HEADS) as h:
            for c in range(CHUNKS):
                split_hi(H0 + 1 + 5 * h, c)
                if c == 3:
                    act.wait_ge(w_arg, h + 1)
                    nc.scalar.activation(W[:], W[:], ACT.Exp).then_inc(w_exp, 1)
            act.wait_ge(h_const, 1)
            to_padded(0, 0, q_ev)
            act.wait_ge(q_ev, 3 * h + 3)
            act.sem_inc(slot_free[0], 1)
            for c in range(CHUNKS):
                split_hi(H0 + 2 + 5 * h, c)
                if c == 0:
                    act.wait_ge(wsb_mm, h + 1)
                    nc.scalar.activation(wsb, ps[:, 4, 0:T], ACT.Copy).then_inc(wsb_set, 1)
                if c == 2:
                    act.wait_ge(conv_step, 16 * h + 8)
                    silu(0, silu_q)
            to_padded(2, 1, k_ev)
            act.wait_ge(k_ev, 3 * h + 3)
            act.sem_inc(slot_free[1], 1)
            for c in range(CHUNKS):
                split_hi(H0 + 3 + 5 * h, c)
                ct_copy(h, c)
                if c == 2:
                    act.wait_ge(conv_step, 16 * h + 16)
                    silu(2, silu_k)
            nc.scalar.activation(vz[:], results(0), ACT.Copy).then_inc(v_ev, 1)
            act.wait_ge(v_ev, h + 1)
            act.sem_inc(slot_free[0], 1)
            for c in range(CHUNKS):
                split_hi(H0 + 4 + 5 * h, c)
                ct_copy(h, 4 + c)
                if c == 2:
                    act.wait_ge(kt_t, h + 1)
                    nc.scalar.activation(ktok[:, 0, :], ps[:, 5, 0:DH], ACT.Identity,
                                         scale=gq[:, 0, ds(h + 64, 1)])
                    nc.scalar.activation(ktok[:, 1, :], ps[:, 5, DH:2 * DH], ACT.Identity,
                                         scale=gq[:, 1, ds(h + 64, 1)]).then_inc(kt_ev, 1)
                if c == 3:
                    act.wait_ge(kvs_t, h + 1)
                    nc.scalar.activation(kst[:], ps[:, 5, 0:DH], ACT.Identity, scale=gq[:, 2, ds(h + 64, 1)])
                    nc.scalar.activation(vst[:], ps[:, 5, DH:2 * DH], ACT.Copy)
                    nc.scalar.activation(ktok[0:S, 2, :], ps[0:S, 5, 0:DH], ACT.Identity,
                                         scale=gq[0:S, 2, ds(h + 64, 1)])
                    nc.scalar.activation(vtok_h[0:S, 2, 0:DH], ps[0:S, 5, DH:2 * DH],
                                         ACT.Copy).then_inc(kvs_ev, 1)
            act.wait_ge(nn_ev, h + 1)
            nc.scalar.activation(og[:], results(1), ACT.Tanh, scale=0.5).then_inc(slot_free[1], 1)
            for c in range(CHUNKS):
                split_hi(H0 + 5 + 5 * h, c)
                if c == 0:
                    act.wait_ge(vt_t, h + 1)
                    nc.scalar.activation(vtok_h[:, 0:2, 0:DH], ps[:, 5, :].rearrange("p (t v) -> p t v", t=2),
                                         ACT.Copy).then_inc(vt_ev, 1)
                    act.wait_ge(inter_mm, 8 * h + 8)
                    nc.scalar.activation(vtok_h[S:2 * S, 2, :], ps[S:2 * S, 4, 0:DH + 1],
                                         ACT.Copy).then_inc(lo_rows, 1)
                if c == 1:
                    act.wait_ge(r_set, h + 1)
                    for t, (n, bank) in enumerate(((P, 6), (P, 7), (S, 4))):
                        nc.scalar.activation(hb[0:n, t, :], ps[0:n, bank, 0:DH], ACT.Square,
                                             scale=r3[0:n, t:t + 1],
                                             accum_out=q3[0:n, t:t + 1]).then_inc(sq_set, 1)
                if c == 2:
                    act.wait_ge(f_set, h + 1)
                    act.wait_ge(sq_set, 3 * h + 3)
                    for t, (n, bank) in enumerate(((P, 6), (P, 7), (S, 4))):
                        last = nc.scalar.activation(hb[0:n, t, :], ps[0:n, bank, 0:DH], ACT.Identity,
                                                    scale=f3[0:n, t:t + 1])
                    last.then_inc(h_set, 1)
            nc.scalar.activation(vz[:], results(0), ACT.Silu).then_inc(z_set, 1)
            act.wait_ge(z_set, h + 1)
            act.sem_inc(slot_free[0], 1)
            act.wait_ge(yf_set, h + 1)
            nc.scalar.activation(yh[:, ds(2 * h, 2), :], yf[:], ACT.Copy).then_inc(ya_hi, 1)
            act.wait_ge(cp_mm, h + 1)
            nc.scalar.activation(cpo[:], ps[:, 5, :].rearrange("p (v k) -> p v k", v=2),
                                 ACT.Copy).then_inc(cp_ev, 1)
            act.wait_ge(cp_ev, h + 1)

        with act.Fori(0, 8) as i:
            for c in range(CHUNKS):
                split_hi(MA0 + 1 + 2 * i, c)
            act.wait_ge(slot_free[1], MA_USE[1] + i)
            act.wait_ge(ya_lo, HEADS)
            nc.scalar.activation(tg[:], results(0), ACT.Tanh, scale=0.5).then_inc(slot_free[0], 1)
            for c in range(CHUNKS):
                split_hi(MA0 + 2 + 2 * i, c)
            act.wait_ge(ma_sum, i + 1)
            nc.scalar.activation(mh[:, ds(2 * i, 2), :], sm[:], ACT.Copy, scale=0.5).then_inc(ma_hi, 1)

        def squares(s, pair):
            act.wait_ge(otok_t, pair + 1)
            for t, (n, bank, at) in enumerate(((P, 4, 0), (P, 4, PW), (S, 5, 0))):
                last = nc.scalar.activation(squared[0:n, t, :], ps[0:n, bank + 2 * s, at:at + PW], ACT.Square,
                                            accum_out=osq[0:n, t, ds(pair, 1)])
            last.then_inc(o_sq, 1)

        def o_body(i, first=False, second=False, last=False):
            for s in range(2):
                for c in range(CHUNKS):
                    if not (last and s == 1):
                        split_hi(O0 + 1 + s + 2 * i, c)
                    if c == 1 and not (first and s == 0):
                        squares(1 - s, 2 * i + s - 1)
                if last and s == 1:
                    act.wait_ge(chunk_done, 4 * PAIRS)
                if not first:
                    act.wait_ge(otok_t, 2 * i + s - 1)
                nc.scalar.activation(vf_o[:, s], results(s), ACT.Copy).then_inc(of_set, 1)
                act.wait_ge(of_set, 2 * i + s + 1)
                act.sem_inc(slot_free[s], 1)

        act.wait_ge(osq_set, 1)
        o_body(0, first=True)
        with act.Fori(1, 3) as i:
            o_body(i)
        o_body(3, last=True)
        squares(1, 7)

    @block.vector
    def _(dve):
        def split_lo(pair, c):
            dve.wait_ge(hi_ready, 4 * pair + c + 1)
            nc.vector.tensor_tensor(wlo[:, c], raw[:, c], whi[:, c].bitcast(F32),
                                    ALU.subtract).then_inc(lo_ready, 1)

        def bc(ap, axis, shape):
            return ap.unsqueeze(axis).broadcast_to(shape)

        nc.vector.memset(stat[:], 1.0).then_inc(const_v, 1)
        dve.wait_ge(const_v, 1)
        dve.wait_ge(x_in[1], 16)
        nc.vector.scalar_tensor_tensor(hb0[:, 1, :], xt[:, 1, :], 1.0, xt[:, 1, :], ALU.mult, ALU.mult,
                                       accum_out=stat[:, 1:2]).then_inc(x_sq, 1)
        dve.wait_ge(x_sq, 3)
        nc.vector.tensor_scalar(stat[:], stat[:], 1.0 / D, EPS, ALU.mult, ALU.add).then_inc(x_var, 1)
        dve.wait_ge(par_t, 1)
        nc.vector.tensor_copy(par0[:], ps[:, 6, 0:P])
        nc.vector.tensor_copy(par1[:], ps[:, 6, P:P + 64])
        nc.vector.tensor_scalar(ghh[:], ps[:, 6, P + 48:P + 64], 0.5, None, ALU.mult).then_inc(par_set, 1)
        dve.wait_ge(x_rstd, 1)
        for cols in HALVES:
            for t in (1, 2):
                n = P if t < 2 else S
                nc.vector.tensor_scalar(hb0[0:n, t, cols], xt[0:n, t, cols], rstd[0:n, t:t + 1], None,
                                        ALU.mult).then_inc(x_norm, 1)
        dve.wait_ge(par_set, 1)
        for k in range(KT):
            if k % CK == 0:
                split_lo(0, k // CK)
            dve.wait_ge(x_hi, k + 1)
            nc.vector.scalar_tensor_tensor(xl[:, k, :], ps[:, x_bank(k), 0:T], par1[:, 32 + k:33 + k],
                                           xh[:, k, :].bitcast(F32), ALU.mult, ALU.subtract).then_inc(x_lo, 1)
        dve.wait_ge(gw_hi, 2)
        for j in range(2):
            nc.vector.tensor_tensor(wg2[:, :, 64 + 32 * j:72 + 32 * j], wg[:, :, 8 * j:8 * j + 8],
                                    wg2[:, :, 32 * j:32 * j + 8].bitcast(F32),
                                    ALU.subtract).then_inc(gw_lo, 1)
        nc.vector.memset(mv[:], 1.0).then_inc(v_var, 1)

        step = Steps(dve, g_dve)
        smp = lambda t: t[:, TP:T].rearrange("p (b t) -> p b t", t=TS)

        def gates_a():
            dve.wait_ge(g_mm, 1)
            dve.wait_ge(gb_in, 64)
            nc.vector.tensor_copy(gi[:], ps[0:8, 4, 0:T])
            step(nc.vector.tensor_copy(gf[:], ps[32:40, 4, 0:T]))
            nc.vector.tensor_tensor(gi[:], gi[:], ps[64:72, 4, 0:T], ALU.add)
            step(nc.vector.tensor_tensor(gf[:], gf[:], ps[96:104, 4, 0:T], ALU.add))
            dve.sem_inc(g_in, 1)
            step(nc.vector.tensor_scalar(gf[:], gf[:], bg[:, 1:2], None, ALU.add))
            nc.vector.scalar_tensor_tensor(gab[:], gf[:], -1.0, gf[:], ALU.mult, ALU.max).then_inc(g_act_in, 1)

        def gates_b():
            dve.wait_ge(g_act, 2)
            step(nc.vector.scalar_tensor_tensor(glf[:], gf[:], 0.0, gln[:], ALU.min, ALU.subtract))
            step(nc.vector.tensor_tensor_scan(gbc[:], r01[:], glf[:], 0.0, ALU.mult, ALU.add))
            step(nc.vector.scalar_tensor_tensor(ga_[:], gi[:], bg[:, 0:1], gbc[:], ALU.add,
                                                ALU.subtract))
            step(nc.vector.tensor_copy(gd1[:], ga_[:]))
            step(nc.vector.tensor_scalar(gd1[:, 0:1], ga_[:, 0:1], 0.0, None, ALU.max))
            step(nc.vector.tensor_tensor(smp(gd1)[:, :, 0:1].squeeze(2), smp(ga_)[:, :, 0:1].squeeze(2), m0[:],
                                         ALU.max))
            step(nc.vector.tensor_tensor_scan(gM[:], rneg[:], gd1[:], 0.0, ALU.add, ALU.max))
            last = smp(gM)[:, :, TS - 1:TS]
            step(nc.vector.scalar_tensor_tensor(gx[:, 0:T], gM[:], -1.0, gbc[:], ALU.mult, ALU.subtract))
            step(nc.vector.tensor_scalar(gx[:, T:T + TP], ga_[:, 0:TP], gM[:, TP - 1:TP], None, ALU.subtract))
            step(nc.vector.tensor_tensor(gx[:, T + TP:2 * T].rearrange("p (b t) -> p b t", t=TS), smp(ga_),
                                         last.broadcast_to([HEADS, NB, TS]), ALU.subtract))
            step(nc.vector.tensor_tensor(gx[:, 2 * T:2 * T + S].rearrange("p (b t) -> p b t", t=TS),
                                         bc(m0[:], 2, [HEADS, NB, TS]), smp(gM), ALU.subtract))
            nc.vector.tensor_tensor(gx[:, 2 * T + S:], m0[:], last.squeeze(2), ALU.subtract
                                    ).then_inc(g_act_in, 1)
            nc.vector.memset(wsr[:].bitcast(F32), 0.0)
            step(nc.vector.memset(nb[:].bitcast(F32), 0.0))
            step(nc.vector.tensor_scalar(nb[0:HEADS, 0:T], gM[:], -1.0, None, ALU.mult))
            nc.vector.scalar_tensor_tensor(nb[LO:LO + HEADS, 0:T], gM[:], -1.0, nb[0:HEADS, 0:T].bitcast(F32),
                                           ALU.mult, ALU.subtract)
            nc.vector.tensor_tensor(gmn[:, 0:1], gbc[:, TP - 1:TP], gM[:, TP - 1:TP], ALU.add)
            step(nc.vector.tensor_tensor(gmn[:, 1:], smp(gbc)[:, :, TS - 1:TS].squeeze(2), last.squeeze(2), ALU.add))

        def gates_c():
            dve.wait_ge(g_act, 3)
            nc.vector.tensor_copy(gqs[0:8, :], ga_[:])
            nc.vector.tensor_copy(gqs[32:40, :], gy[:, 0:T])
            step(nc.vector.tensor_scalar(gqs[64:72, :], gy[:, T:2 * T], DH ** -0.5, None, ALU.mult))
            step(nc.vector.tensor_scalar(wsr[0:HEADS, :], gy[:, T:2 * T], DH ** -0.5, None, ALU.mult))
            nc.vector.scalar_tensor_tensor(wsr[LO:LO + HEADS, :], gy[:, T:2 * T], DH ** -0.5,
                                           wsr[0:HEADS, :].bitcast(F32), ALU.mult, ALU.subtract)
            nc.vector.tensor_copy(gqs4[:].rearrange("p (n s) -> p n s", s=S), bc(gqs[:, TP:T], 1, [96, P // S, S]))
            step(nc.vector.tensor_copy(nb[0:HEADS, T:], gy[:, 2 * T:2 * T + S]))
            nc.vector.tensor_tensor(nb[LO:LO + HEADS, T:], gy[:, 2 * T:2 * T + S], nb[0:HEADS, T:].bitcast(F32),
                                    ALU.subtract)
            nc.vector.tensor_tensor(gdx[:], bc(gy[:, 2 * T + S:], 1, [HEADS, HEADS, NB]),
                                    bc(eye8[0:HEADS], 2, [HEADS, HEADS, NB]), ALU.mult).then_inc(g_rows, 1)

        def gates_d():
            n_turned = ps[:, 7, 384:512].rearrange("p (k n) -> p k n", k=2)
            dve.wait_ge(g_t, 1)
            nc.vector.tensor_copy(gq[:, 0:2, :], ps[:, 5, 256:448].rearrange("p (t q) -> p t q", t=2))
            nc.vector.tensor_copy(dec_bc[:], ps[:, 5, 448:512])
            nc.vector.tensor_copy(gq[:, 2, :], ps[:, 7, 256:352])
            step(nc.vector.tensor_copy(nTh[:], n_turned))
            nc.vector.tensor_tensor(nacc[:, :, 0:NB, :], n_turned.rearrange("p k (b h) -> p k b h", h=HEADS),
                                    bc(dec_bc[:].rearrange("p (h b) -> p b h", b=NB), 1, [P, 2, NB, HEADS]),
                                    ALU.mult)
            nc.vector.tensor_tensor(nTl[:], n_turned, nTh[:].bitcast(F32), ALU.subtract).then_inc(g_set, 1)

        def w_s_masked():
            dve.wait_ge(ws_t, 1)
            dve.wait_ge(consts, 2)
            nc.vector.tensor_copy(rep4[:].rearrange("p (b t) -> p b t", t=TS),
                                  bc(ident[0:TS, 0:TS], 1, [TS, NB, TS]))
            for q in range(2):
                nc.vector.tensor_tensor(wsT[:, 4 * q:4 * q + 4, :],
                                        ps[:, 6 + q, :].rearrange("p (g t) -> p g t", g=4),
                                        bc(tri01[:], 1, [P, 4, P]), ALU.mult).then_inc(ws_set, 1)

        def w_s_blocks():
            dve.wait_ge(ws_t, 2)
            nc.vector.tensor_tensor(wd[:].rearrange("p g (b t) -> p g b t", t=TS),
                                    bc(ps[0:S, 6, 0:S].rearrange("p (g t) -> p g t", t=TS), 2, [S, GROUPS, NB, TS]),
                                    bc(blk01[:].rearrange("p (b t) -> p b t", t=TS), 1, [S, GROUPS, NB, TS]),
                                    ALU.mult).then_inc(ws_set, 1)

        def from_turned(s, pair, col):
            dve.wait_ge(tok_t, pair + 1)
            b = 4 + 2 * s
            for t in range(2):
                nc.vector.bn_stats(vstat[:, t, ds(pair, 1), :], ps[:, b, PW * t:PW * t + PW])
            nc.vector.bn_stats(vstat[0:S, 2, ds(pair, 1), :], ps[0:S, b + 1, 0:PW])
            nc.vector.tensor_copy(vtok[:, 0:2, ds(col, PW)], ps[:, b, :].rearrange("p (t v) -> p t v", t=2))
            nc.vector.tensor_copy(vtok[0:S, 2, ds(col, PW)], ps[0:S, b + 1, 0:PW]).then_inc(tok_ev, 1)

        def v_body(i, small={}):
            for s in range(2):
                for c in range(CHUNKS):
                    split_lo(V0 + 1 + s + 2 * i, c)
                    if c == 1 and (s, c, 0) not in small:
                        from_turned(1 - s, 2 * i + s - 1, 2 * PW * i + PW * (s - 1))
                    for f in small.get((s, c), ()):
                        f()

        v_body(0, {(0, 1, 0): (), (0, 3): (gates_a,), (1, 0): (w_s_masked,), (1, 2): (w_s_blocks,)})
        v_body(1, {(0, 0): (gates_b,), (0, 3): (gates_c,), (1, 3): (gates_d,)})
        with dve.Fori(2, 4) as i:
            v_body(i)

        def layer_norm_stats():
            dve.wait_ge(tok_ev, 8)
            dve.wait_ge(v_var, 1)
            for t in range(3):
                n = P if t < 2 else S
                nc.vector.bn_aggr(mv[0:n, t, :], vstat[0:n, t].rearrange("p a b -> p (a b)")).then_inc(v_var, 1)
            dve.wait_ge(v_var, 4)
            nc.vector.tensor_scalar(stat[:], mv[:, :, 1:2].squeeze(2), EPS, None, ALU.add).then_inc(v_var, 1)
            nc.vector.tensor_scalar(nmu[:], mv[:, :, 0:1].squeeze(2), -1.0, None, ALU.mult).then_inc(v_var, 1)

        def g_body(i, first=False):
            if first:
                split_lo(G0 + 1, 0)
                from_turned(1, 7, 7 * PW)
                layer_norm_stats()
            if not first:
                dve.wait_ge(sp_mm, i)
                dve.wait_ge(vr_out, 32 * i)
            else:
                dve.wait_ge(v_rstd, 1)
                dve.wait_ge(v_var, 6)
                dve.wait_ge(ln_in, 32)
            vstep = Steps(dve, vn_step, 2 * i)
            col = ds(DH * i, DH)
            for t in range(3):
                n = P if t < 2 else S
                ins = nc.vector.tensor_scalar(vn[0:n, t, :], vtok[0:n, t, col], nmu[0:n, t:t + 1],
                                              rstd[0:n, t:t + 1], ALU.add, ALU.mult)
            vstep(ins)
            nc.vector.tensor_tensor(vn[:, 0:2, :], vn[:, 0:2, :], bc(lng[:, col], 1, [P, 2, DH]), ALU.mult)
            vstep(nc.vector.tensor_tensor(vn[0:S, 2, :], vn[0:S, 2, :], lng[0:S, col], ALU.mult))
            nc.vector.tensor_tensor(vn[:, 0:2, :], vn[:, 0:2, :], bc(lnb[:, col], 1, [P, 2, DH]), ALU.add)
            nc.vector.tensor_tensor(vn[0:S, 2, :], vn[0:S, 2, :], lnb[0:S, col], ALU.add).then_inc(vn_ready, 1)
            for c in range(1 if first else 0, CHUNKS):
                split_lo(G0 + 1 + 2 * i, c)
            for c in range(CHUNKS):
                split_lo(G0 + 2 + 2 * i, c)
                if c == 0:
                    dve.wait_ge(sp_mm, i + 1)
                    dve.wait_ge(slot_free[0], G_USE[0] + i + 1)
                    nc.vector.tensor_tensor(tt_g[:, :, 0:TP].rearrange("p j (n t) -> p j n t", t=P),
                                            ps[:, 4:6, 0:TP].rearrange("p j (n t) -> p j n t", t=P),
                                            bsb[:, ds(i, 1), :].unsqueeze(1).broadcast_to([P, 2, 2, P]), ALU.add)
                    nc.vector.tensor_tensor(tt_g[:, :, TP:T].rearrange("p j (n t) -> p j n t", t=TS),
                                            ps[:, 4:6, TP:T].rearrange("p j (n t) -> p j n t", t=TS),
                                            bsb[:, ds(i, 1), 0:TS].unsqueeze(1).broadcast_to([P, 2, NB, TS]),
                                            ALU.add).then_inc(sp_used, 1)
                    dve.wait_ge(sp_used, i + 1)
                    nc.vector.tensor_tensor(tt_g[:], tt_g[:], uf[:], ALU.mult).then_inc(tt_set, 1)
            dve.wait_ge(slot_free[1], G_USE[1] + i + 1)
            dve.wait_ge(tt_set, i + 1)
            nc.vector.tensor_tensor(yf_g[:], tt_g[:], zs_g[:], ALU.mult).then_inc(yg_ready, 1)
            dve.wait_ge(yg_hi, i + 1)
            nc.vector.tensor_tensor(yl[:, ds(2 * i, 2), :], yf_g[:], yh[:, ds(2 * i, 2), :].bitcast(F32),
                                    ALU.subtract).then_inc(yg_lo, 1)

        g_body(0, first=True)
        with dve.Fori(1, GROUPS) as i:
            g_body(i)

        with dve.Fori(0, 8) as i:
            for j in range(2):
                for c in range(CHUNKS):
                    split_lo(MB0 + 1 + j + 2 * i, c)
            dve.wait_ge(slot_free[0], MB_USE[0] + i + 1)
            dve.wait_ge(chunk_done, 4 * MB0 + 8 + 8 * i)
            nc.vector.scalar_tensor_tensor(part[:, ds(2 * i, 2), :], tg[:], 1.0, ps[:, 2:4, 0:T], ALU.add,
                                           ALU.mult).then_inc(slot_free[1], 1)

        dve.wait_ge(vr_out, 32 * GROUPS)
        nc.vector.memset(qm[:].bitcast(F32), 0.0)
        nc.vector.memset(CTh[:].bitcast(F32), 0.0)
        nc.vector.memset(CTl[:].bitcast(F32), 0.0)
        nc.vector.memset(xp[:, :, 0:HIST], 0.0)
        nc.vector.memset(vtok_h[:, :, DH:DH + 1], 1.0)
        nc.vector.memset(r3[:], 1.0)
        nc.vector.memset(q3[:], 1.0)
        nc.vector.memset(f3[:], 1.0)
        nc.vector.memset(W[:], 0.0)
        nc.vector.memset(ones8h[:].bitcast(F32), 1.0).then_inc(h_const, 1)
        dve.wait_ge(h_const, 1)

        def conv(h, j, blk, taps):
            for tap in taps:
                for jj in range(2):
                    w_at = par0[:, ds(2 * h + (32 * tap + blk + jj), 1)]
                    out, src = acc[:, jj, 0:CW], xp[:, j + jj, tap:tap + CW]
                    if tap == 0:
                        ins = nc.vector.tensor_scalar(out, src, w_at, par1[:, ds(2 * h + (blk + jj), 1)],
                                                      ALU.mult, ALU.add)
                    else:
                        dve.wait_ge(conv_step, 16 * h + (4 * j + 2 * tap + jj - 1))
                        ins = nc.vector.scalar_tensor_tensor(out, src, w_at, out, ALU.mult, ALU.add)
                    ins.then_inc(conv_step, 1)

        def own(part_):
            return qm[:, :, part_:part_ + NB * (2 * S + TS)].rearrange(
                "p k (b x) -> p k b x", x=2 * S + TS)[:, :, :, 0:TS]

        def ct_split(h, b):
            dve.wait_ge(ct_ev, 8 * h + b + 1)
            for t, n in ((CTh, nTh), (CTl, nTl)):
                nc.vector.tensor_copy(t[:, :, DH:DH + 1], n[:, :, ds(h + 8 * b, 1)].bitcast(F32))
            nc.vector.tensor_tensor(key_major(CTl), turned(b), key_major(CTh).bitcast(F32),
                                    ALU.subtract).then_inc(ct_lo, 1)

        def of_sequence(h, b):
            if b >= 4:
                dve.wait_ge(cs_mm, 8 * h + b - 3)
            nc.vector.tensor_scalar(vm[:, b % 4, :], vst[:].bitcast(F32), mask8[:, b:b + 1], None,
                                    ALU.mult).then_inc(vm_set, 1)

        def add_state(h, b):
            dve.wait_ge(cs_mm, 8 * h + b + 1)
            nc.vector.scalar_tensor_tensor(Cin[:, b], Cin[:, b], dec_bc[:, ds(8 * h + b, 1)],
                                           ps[:, NEW_BANK[b % 3], :].rearrange("p (v k) -> p v k", v=2),
                                           ALU.mult, ALU.add).then_inc(cs_ev, 1)

        with dve.Fori(0, HEADS) as h:
            nc.vector.tensor_scalar(bcrow[:], nb[:].bitcast(F32), eye8[:, ds(h, 1)], None, ALU.mult).then_inc(bc_row, 1)
            for c in range(CHUNKS):
                split_lo(H0 + 1 + 5 * h, c)
                if c == 1:
                    dve.wait_ge(hist_t, h + 1)
                    for j in range(4):
                        last = nc.vector.tensor_copy(
                            xp[:, j, XPS:XPW].rearrange("p (b t) -> p b t", t=HIST + TS)[:, :, 0:HIST],
                            ps[:, 4, 24 * j:24 * j + 24].rearrange("p (b t) -> p b t", t=HIST))
                    last.then_inc(hist_set, 1)
                if c == 2:
                    dve.wait_ge(bc_mm, h + 1)
                    nc.vector.tensor_copy(scb[:], bc(ps[:, 5, T:T + S], 1, [P, 2, S]))
                    nc.vector.tensor_scalar(W[:, P:TP], ps[:, 5, P:TP], gq[:, 0, ds(h, 1)], None, ALU.add)
                    for t, (lo, n, at, mask) in enumerate(((0, P, 0, 0), (P, P, TP, 0), (TP, S, 384, P))):
                        last = nc.vector.scalar_tensor_tensor(
                            W[:, at:at + n], ps[:, 5, lo:lo + n], gq[:, t, ds(h, 1)], keep_w[:, mask:mask + n],
                            ALU.add, ALU.min)
                    last.then_inc(w_arg, 1)
                    nc.vector.tensor_scalar(bcrow[:, 0:T], wsr[:].bitcast(F32), eye8[:, ds(h, 1)], None,
                                            ALU.mult).then_inc(ws_row, 1)
            for c in range(CHUNKS):
                split_lo(H0 + 2 + 5 * h, c)
                if c == 0:
                    dve.wait_ge(q_ev, 3 * h + 3)
                    dve.wait_ge(hist_set, h + 1)
                    conv(h, 0, 0, (0, 1))
                if c == 1:
                    conv(h, 0, 0, (2, 3))
                if c == 3:
                    dve.wait_ge(silu_q, 3 * h + 3)
                    qs = Steps(dve, q_step, 2 * h)
                    qs(nc.vector.tensor_tensor(scb[:], qk[:, 0:2, TP:T], scb[:], ALU.mult))
                    scaled = scb[:].rearrange("p k (b t) -> p k b t", t=TS)
                    qs(nc.vector.tensor_copy(own(0), scaled))
                    last = nc.vector.tensor_tensor(own(S), scaled, own(0).bitcast(F32), ALU.subtract)
                    last.then_inc(qm_set, 1)
            for c in range(CHUNKS):
                split_lo(H0 + 3 + 5 * h, c)
                ct_split(h, c)
                if c == 0:
                    dve.wait_ge(k_ev, 3 * h + 3)
                    conv(h, 2, 16, (0, 1))
                if c == 1:
                    conv(h, 2, 16, (2, 3))
                if c == 2:
                    nc.vector.tensor_copy(cn[:, :, 0:3], xp[:, :, TP:XPS])
                    for j in range(4):
                        last = nc.vector.tensor_copy(
                            cn[:, j, 3:27].rearrange("p (b t) -> p b t", t=3),
                            xp[:, j, XPS:XPW].rearrange("p (b t) -> p b t", t=HIST + TS)[:, :, TS:])
                    last.then_inc(cn_set, 1)
                if c == 3:
                    dve.wait_ge(silu_k, 3 * h + 3)
                    nc.vector.tensor_copy(kv4[:, 0].rearrange("p j (n s) -> p j n s", s=S),
                                          bc(qk[:, 2:4, TP:T], 2, [P, 2, P // S, S])).then_inc(kv4_set, 1)
                    dve.wait_ge(wsb_set, h + 1)
                    for j in range(2):
                        nc.vector.scalar_tensor_tensor(
                            acc[:, j, 0:TP], qk[:, 2 + j, 0:TP], 1.0, wsb[:, 0:TP], ALU.mult, ALU.mult,
                            accum_out=nacc[:, j, NB, ds(h, 1)])
                    ns = Steps(dve, n_step, 2 * h)
                    ns(nc.vector.tensor_tensor(scb[:], qk[:, 2:4, TP:T], bc(wsb[:, TP:T], 1, [P, 2, S]), ALU.mult))
                    added = og[:, 1, TP:TP + 2 * NB].rearrange("p (k b) -> p k b", k=2)
                    ns(nc.vector.tensor_reduce(added, scb[:].rearrange("p k (b t) -> p k b t", t=TS),
                                               mybir.AxisListType.X, ALU.add))
                    of_head = nacc[:, :, 0:NB, ds(h, 1)].squeeze(3)
                    nc.vector.tensor_tensor(of_head, of_head, added, ALU.add).then_inc(nn_ev, 1)
            for c in range(CHUNKS):
                split_lo(H0 + 4 + 5 * h, c)
                if c == 2:
                    dve.wait_ge(v_ev, h + 1)
                    nc.vector.tensor_copy(kv4[:, 1].rearrange("p j (n s) -> p j n s", s=S),
                                          bc(vz[:, :, TP:T], 2, [P, 2, P // S, S])).then_inc(kv4_set, 1)
                ct_split(h, 4 + c)
                if c == 0:
                    dve.wait_ge(s_mm, h + 1)
                    dve.wait_ge(w_exp, h + 1)
                    nc.vector.scalar_tensor_tensor(W[:, 0:384], ps[:, 5, 0:384], DH ** -0.5, W[:, 0:384],
                                                   ALU.mult, ALU.mult)
                    nc.vector.tensor_copy(W[S:2 * S, 384:416], ident[S:2 * S, S:2 * S])
                    nc.vector.scalar_tensor_tensor(W[0:S, 384:416], ps[0:S, 5, 384:416], DH ** -0.5,
                                                   W[0:S, 384:416], ALU.mult, ALU.mult).then_inc(p_set, 1)
                if c == 1:
                    dve.wait_ge(cn_t, h + 1)
                    nc.vector.tensor_copy(cst[:].rearrange("p a b -> p (a b)"), ps[0:27, 5, :]).then_inc(cst_ev, 1)
                if c == 3:
                    dve.wait_ge(kvs_ev, h + 1)
                    for rows in (slice(S, 2 * S), slice(3 * S, P)):
                        nc.vector.scalar_tensor_tensor(kst[rows], ps[rows, 5, 0:DH], gq[rows, 2, ds(h + 64, 1)],
                                                       kst[rows].bitcast(F32), ALU.mult, ALU.subtract)
                    nc.vector.tensor_tensor(vst[2 * S:P], ps[2 * S:P, 5, DH:2 * DH], vst[2 * S:P].bitcast(F32),
                                            ALU.subtract).then_inc(st_lo, 1)
                    dve.wait_ge(st_lo, h + 1)
                    for b in range(4):
                        of_sequence(h, b)
            for c in range(CHUNKS):
                split_lo(H0 + 5 + 5 * h, c)
                if c == 0:
                    add_state(h, 0)
                    of_sequence(h, 4)
                    add_state(h, 1)
                    of_sequence(h, 5)
                if c == 1:
                    dve.wait_ge(num_mm, h + 1)
                    for t, (n, bank) in enumerate(((P, 6), (P, 7), (S, 4))):
                        last = nc.vector.tensor_copy(f3[0:n, t:t + 1], ps[0:n, bank, DH:DH + 1])
                    den = Steps(dve, den_step, 3 * h)
                    den(last)
                    den(nc.vector.scalar_tensor_tensor(q3[:], f3[:], -1.0, f3[:], ALU.mult, ALU.max))
                    den(nc.vector.tensor_tensor(q3[:], q3[:], gq[:, :, ds(h + 32, 1)].squeeze(2), ALU.max))
                    nc.vector.reciprocal(r3[:], q3[:]).then_inc(r_set, 1)
                    add_state(h, 2)
                    of_sequence(h, 6)
                    dve.wait_ge(sq_set, 3 * h + 3)
                    nc.vector.tensor_scalar(stat[:], q3[:], 1.0 / DH, EPS, ALU.mult, ALU.add).then_inc(var_set, 1)
                    add_state(h, 3)
                    of_sequence(h, 7)
                    dve.wait_ge(rs_set, h + 1)
                    nc.vector.tensor_tensor(f3[:], r3[:], rstd[:], ALU.mult).then_inc(f_set, 1)
                if c == 2:
                    add_state(h, 4)
                    add_state(h, 5)
            dve.wait_ge(z_set, h + 1)
            dve.wait_ge(slot_free[1], H_USE[1] + 2 + 2 * h)
            nc.vector.scalar_tensor_tensor(og[:], og[:], 1.0, vz[:], ALU.add, ALU.mult).then_inc(gate_set, 1)
            dve.wait_ge(gate_set, h + 1)
            dve.wait_ge(ht_t, h + 1)
            for j in range(2):
                last = nc.vector.scalar_tensor_tensor(yf[:, j, :], ps[:, 6 + j, 0:T], ghh[:, ds(2 * h + j, 1)],
                                                      og[:, j, :], ALU.mult, ALU.mult)
            last.then_inc(yf_set, 1)
            dve.wait_ge(ya_hi, h + 1)
            nc.vector.tensor_tensor(yl[:, ds(2 * h, 2), :], yf[:], yh[:, ds(2 * h, 2), :].bitcast(F32),
                                    ALU.subtract).then_inc(ya_lo, 1)
            for b in range(6, NB):
                add_state(h, b)
            dve.wait_ge(cs_ev, 8 * h + 8)

        def left():
            for s, n in ((cs_out[0], 8), (cs_out[1], 8), (cp_out, 8), (cst_out, 16)):
                dve.wait_ge(s, 16 * n)

        with dve.Fori(0, 8) as i:
            for j in range(2):
                for c in range(CHUNKS):
                    split_lo(MA0 + 1 + j + 2 * i, c)
            dve.wait_ge(slot_free[0], MA_USE[0] + i + 1)
            dve.wait_ge(chunk_done, 4 * MA0 + 8 + 8 * i)
            left()
            nc.vector.scalar_tensor_tensor(tm[:], tg[:], 1.0, ps[:, 2:4, 0:T], ALU.add,
                                           ALU.mult).then_inc(slot_free[1], 1)
            dve.wait_ge(slot_free[1], MA_USE[1] + i + 1)
            nc.vector.tensor_tensor(sm[:], tm[:], part[:, ds(2 * i, 2), :], ALU.add).then_inc(ma_sum, 1)
            dve.wait_ge(ma_hi, i + 1)
            nc.vector.scalar_tensor_tensor(ml[:, ds(2 * i, 2), :], sm[:], 0.5,
                                           mh[:, ds(2 * i, 2), :].bitcast(F32), ALU.mult,
                                           ALU.subtract).then_inc(ma_lo, 1)

        def from_turned_o(s, pair, col):
            dve.wait_ge(o_sq, pair + 1)
            b = 4 + 2 * s
            nc.vector.tensor_tensor(otok[:, 0:2, ds(col, PW)], ps[:, b, :].rearrange("p (t v) -> p t v", t=2),
                                    bc(gpost[:, ds(col, PW)], 1, [P, 2, PW]), ALU.mult)
            nc.vector.tensor_tensor(otok[0:S, 2, ds(col, PW)], ps[0:S, b + 1, 0:PW], gpost[0:S, ds(col, PW)],
                                    ALU.mult).then_inc(otok_ev, 1)

        def o_body(i, first=False, last=False):
            for s in range(2):
                for c in range(CHUNKS):
                    if not (last and s == 1):
                        split_lo(O0 + 1 + s + 2 * i, c)
                    if c == 1 and not (first and s == 0):
                        if first:
                            dve.wait_ge(g_post_in, 16)
                        from_turned_o(1 - s, 2 * i + s - 1, 2 * PW * i + PW * (s - 1))
                    if first and (s, c) == (1, 3):
                        dve.wait_ge(n_turn, 1)
                        nc.vector.tensor_copy(nout[:], ps[0:(NB + 1) * HEADS, 6, 0:DH]).then_inc(n_rows, 1)

        nc.vector.memset(osq[:], 1.0).then_inc(osq_set, 1)
        o_body(0, first=True)
        with dve.Fori(1, 3) as i:
            o_body(i)
        o_body(3, last=True)
        from_turned_o(1, 7, 7 * PW)
        nc.vector.tensor_reduce(stat[:], osq[:], mybir.AxisListType.X, ALU.add).then_inc(o_var, 1)
        dve.wait_ge(o_var, 1)
        nc.vector.tensor_scalar(stat[:], stat[:], 1.0 / D, EPS, ALU.mult, ALU.add).then_inc(o_var, 1)
        dve.wait_ge(o_rstd, 1)
        dve.wait_ge(otok_ev, 8)
        dve.wait_ge(x_again, 32)
        for n, t, cols in Y_PARTS:
            nc.vector.scalar_tensor_tensor(otok[0:n, t, cols], otok[0:n, t, cols], rstd[0:n, t:t + 1],
                                           xres[0:n, t, cols], ALU.mult, ALU.add).then_inc(y_set, 1)

    @block.gpsimd
    def _(pool):
        step = Steps(pool, pool_step)
        step(nc.gpsimd.memset(ident[:], 0.0))
        nc.gpsimd.affine_select(out=ident[:], in_=ident[:], compare_op=ALU.not_equal, fill=1.0, base=0,
                                pattern=[[-1, P]], channel_multiplier=1).then_inc(consts, 1)
        nc.gpsimd.memset(half[:], -0.5)
        nc.gpsimd.memset(keep_w[:], 0.0)
        nc.gpsimd.memset(mask8[:], 1.0)
        nc.gpsimd.memset(eye8[:], 0.0)
        nc.gpsimd.memset(gq[:], 0.0)
        nc.gpsimd.memset(wg2[:].bitcast(F32), 0.0)
        nc.gpsimd.memset(r01[:], 1.0)
        nc.gpsimd.memset(rneg[:], 0.0)
        nc.gpsimd.memset(gqs[:], 0.0)
        step(nc.gpsimd.memset(ones8[:], 1.0))
        pool.sem_inc(gw_zero, 1)

        def select(out, pattern, base, cm, fill, op=ALU.is_ge):
            step(nc.gpsimd.affine_select(out=out, in_=out, compare_op=op, fill=fill, base=base,
                                         pattern=pattern, channel_multiplier=cm))

        select(keep_w[:, 0:P], [[1, P]], 0, -1, MASKED)
        select(keep_w[:, P:], [[1, S]], 0, -1, MASKED)
        select(keep_w[:, P:].rearrange("p (b t) -> p b t", t=TS), [[-TS, NB], [0, TS]], 0, 1, MASKED)
        for g4 in range(0, P, S):
            select(mask8[g4:g4 + S], [[-TS, NB]], 0, 1, 0.0)
            select(mask8[g4:g4 + S], [[TS, NB]], TS - 1, -1, 0.0)
        for row in (0, LO):
            select(eye8[row:row + HEADS], [[-1, HEADS]], 0, 1, 1.0, ALU.not_equal)
        for t, v in ((r01, 0.0), (rneg, NEVER)):
            nc.gpsimd.memset(t[:, 0:1], v)
            nc.gpsimd.memset(t[:, TP:T].rearrange("p (b t) -> p b t", t=TS)[:, :, 0:1], v)
        pool.dma_start(wg[:], w_in.rearrange("(k p) n -> p k n", p=P)[:, :, COL_IG:COL_IG + 16]).then_inc(gin, 16)
        pool.wait_ge(x_var, 1)
        nc.gpsimd.tensor_tensor(rstd[:], stat[:], half[:], ALU.pow).then_inc(x_rstd, 1)
        pool.dma_start(bg[:, 0:1], b_ig.unsqueeze(1)).then_inc(gb_in, 16)
        pool.dma_start(bg[:, 1:2], b_fg.unsqueeze(1)).then_inc(gb_in, 16)
        with nc.allow_non_contiguous_dma(reason="64 values"):
            pool.dma_start(m0[:], state_m.rearrange("b h -> h b")).then_inc(gb_in, 16)
        pool.dma_start(nrow[:], state_n.rearrange("b h d -> (b h) d")).then_inc(gb_in, 16)
        pool.wait_ge(x_t, KT)
        nc.gpsimd.memset(tri01[:], 1.0)
        step(nc.gpsimd.memset(blk01[:], 1.0))
        select(tri01[:], [[1, P]], 0, -1, 0.0)
        select(blk01[:], [[1, S]], 0, -1, 0.0)
        nc.gpsimd.affine_select(out=blk01[:].rearrange("p (b t) -> p b t", t=TS),
                                in_=blk01[:].rearrange("p (b t) -> p b t", t=TS), compare_op=ALU.is_ge,
                                fill=0.0, base=0, pattern=[[-TS, NB], [0, TS]],
                                channel_multiplier=1).then_inc(consts, 1)
        pool.dma_start(wsn[:], w_s.rearrange("g t s -> t g s")).then_inc(w_sp_in, 16)
        pool.dma_start(bsb[:].rearrange("p g t -> p (g t)"), b_s.rearrange("g t -> (g t)").partition_broadcast(P)
                       ).then_inc(w_sp_in, 16)
        pool.dma_start(lng[:], ln_g.partition_broadcast(P)).then_inc(ln_in, 16)
        pool.dma_start(lnb[:], ln_b.partition_broadcast(P)).then_inc(ln_in, 16)
        pool.wait_ge(g_rows, 1)
        with nc.allow_non_contiguous_dma(reason="72 values"):
            pool.dma_start(m_p.rearrange("o h -> h o"), gmn[:, 0:1]).then_inc(m_out, 16)
            pool.dma_start(m_s.rearrange("b h -> h b"), gmn[:, 1:]).then_inc(m_out, 16)
        pool.wait_ge(v_var, 6)
        nc.gpsimd.tensor_tensor(rstd[:], stat[:], half[:], ALU.pow).then_inc(v_rstd, 1)
        with pool.Fori(0, GROUPS) as i:
            pool.wait_ge(vn_ready, i + 1)
            pool.nop(nofuse=True)
            pool.dma_start(vrows_p[0, :, ds(DH * i, DH)], vn[:, 1, :]).then_inc(vr_out, 16)
            pool.dma_start(vrows_s.rearrange("b t d -> (b t) d")[:, ds(DH * i, DH)], vn[0:S, 2, :]
                           ).then_inc(vr_out, 16)

        def load_c(h, half_):
            pool.dma_start(Cin[:, 4 * half_:4 * half_ + 4].rearrange("p b v k -> p b (v k)"),
                           Cs_in[:, 4 * half_:4 * half_ + 4, ds(h, 1)].rearrange("p b o n -> p (b o) n")).then_inc(c_in[half_], 16)

        def load_hist(h):
            pool.dma_start(hst[:], conv_in_v[:, :, ds(DH * h, DH)]).then_inc(hst_in, 16)

        pool.wait_ge(yg_lo, GROUPS)
        pool.wait_ge(tt_set, GROUPS)
        pool.wait_ge(vr_out, 32 * GROUPS)
        load_c(0, 0)
        load_c(0, 1)
        load_hist(0)

        def h_body(h, more=True):
            pool.wait_ge(cst_ev, h + 1)
            pool.nop(nofuse=True)
            for rows, out in ((slice(0, 3), conv_p_v), (slice(3, 27), conv_s_v)):
                pool.dma_start(out[:, :, ds(DH * h, DH)], cst[rows].rearrange("r (s a) b -> r s (a b)", s=2)
                               ).then_inc(cst_out, 16)
            if more:
                load_hist(h + 1)
            pool.wait_ge(var_set, h + 1)
            nc.gpsimd.tensor_tensor(rstd[:], stat[:], half[:], ALU.pow).then_inc(rs_set, 1)
            pool.wait_ge(cp_ev, h + 1)
            pool.nop(nofuse=True)
            pool.dma_start(Cp_out[:, ds(h, 1)].rearrange("p o n -> p (o n)"),
                           cpo[:].rearrange("p v k -> p (v k)")).then_inc(cp_out, 16)
            for half_ in range(2):
                pool.wait_ge(cs_ev, 8 * h + 4 * half_ + 4)
                pool.nop(nofuse=True)
                pool.dma_start(Cs_out[:, 4 * half_:4 * half_ + 4, ds(h, 1)].rearrange("p b o n -> p (b o) n"),
                               Cin[:, 4 * half_:4 * half_ + 4].rearrange("p b v k -> p b (v k)")).then_inc(cs_out[half_], 16)
            if more:
                pool.wait_ge(cst_out, 32 * h + 32)
                pool.wait_ge(cp_out, 16 * h + 16)
                for half_ in range(2):
                    pool.wait_ge(cs_out[half_], 16 * h + 16)
                    pool.nop(nofuse=True)
                    load_c(h + 1, half_)

        with pool.Fori(0, HEADS - 1) as h:
            h_body(h)
        h_body(HEADS - 1, more=False)
        pool.wait_ge(n_rows, 1)
        pool.dma_start(n_s.rearrange("b h k -> (b h) k"), nout[0:NB * HEADS, :]).then_inc(nn_out, 16)
        pool.dma_start(n_p[0], nout[NB * HEADS:(NB + 1) * HEADS, :]).then_inc(nn_out, 16)
        pool.wait_ge(o_var, 2)
        nc.gpsimd.tensor_tensor(rstd[:], stat[:], half[:], ALU.pow).then_inc(o_rstd, 1)
        for s, n in ((m_out, 2), (vr_out, 16), (cst_out, 16), (nn_out, 2), (cp_out, 8), (cs_out[0], 8),
                     (cs_out[1], 8)):
            pool.wait_ge(s, 16 * n)

    block.__exit__(None, None, None)


_INS = ["x_prompt", "x_sample", "state_mlstm_C", "state_mlstm_n", "state_mlstm_m", "state_conv_qk", "g_pre", "w_in",
        "b_ig", "b_fg", "w_conv", "b_conv", "g_head", "ln_g", "ln_b", "w_s", "b_s", "w_pa", "w_pb", "w_out", "g_post"]
_OUTS = [(1, TP, D), (NB, TS, D), (1, HEADS, DH, DH), (1, HEADS, DH), (1, HEADS), (1, HIST, 2 * D), (1, P, D),
         (NB, HEADS, DH, DH), (NB, HEADS, DH), (NB, HEADS), (NB, HIST, 2 * D), (NB, TS, D)]


def kernel(**inputs):
    import numpy as np
    import concourse.bacc as bacc
    from concourse.bass_utils import run_bass_kernel_spmd

    nc = bacc.Bacc("TRN2", target_bir_lowering=False, num_devices=1)
    arrays, args = {}, []
    for name in _INS:
        arr = np.ascontiguousarray(inputs[name])
        arrays[f"in_{name}_dram"] = arr
        args.append(nc.dram_tensor(f"in_{name}_dram", arr.shape, mybir.dt.from_np(arr.dtype),
                                   kind="ExternalInput").ap())
    for n, shape in enumerate(_OUTS):
        args.append(nc.dram_tensor(f"out_{n}_dram", shape, F32, kind="ExternalOutput").ap())
    build(nc, *args)
    r = run_bass_kernel_spmd(nc, [arrays], core_ids=[0])
    return tuple(r.results[0][f"out_{n}_dram"] for n in range(len(_OUTS)))
```
